# Optimizing a Trainium2 kernel written in Bass

```python
import math
import jax, jax.numpy as jnp
from jax import lax
import numpy as np

D_MODEL = 1024
BATCH = 1
SEQ = 512
DEPTH = 2
DEC_BATCH = 8
DEC_SEQ = 4
PAST_LEN = 1024
PAGE_SIZE = 128

W_CONV = D_MODEL // 4
W_POOL = D_MODEL // 4
W_ATTN = D_MODEL - W_CONV - W_POOL
N_HEADS = 8
HEAD_DIM = W_ATTN // N_HEADS
CONV_WIDTH = 3
POOL_WINDOWS = (2, 4, 8, 16)
POOL_GROUP = W_POOL // len(POOL_WINDOWS)
POOL_PREV = max(POOL_WINDOWS) - 1
IDX_HEADS = 8
IDX_DIM = 64
TOPK_MAX = 256
NUM_BUCKETS = 32
MAX_DISTANCE = 128
D_FF = ((8 * D_MODEL // 3 + 127) // 128) * 128
Q_BLOCK = 128
EPS = 1e-6
SPLITS = (W_CONV, W_CONV, W_CONV, W_POOL, W_ATTN, W_ATTN, W_ATTN, IDX_HEADS * IDX_DIM, IDX_DIM, IDX_HEADS)
D_IN = sum(SPLITS)

kernel_name = "hymba_conv_pool_dsa_macaron_step"

def _rmsnorm(x, g):
    xf = x.astype(jnp.float32)
    xf = xf * lax.rsqrt(jnp.mean(xf * xf, axis=-1, keepdims=True) + EPS)
    return (xf * g.astype(jnp.float32)).astype(x.dtype)

def _swiglu(h, wg, wu, wd):
    return (jax.nn.silu(h @ wg) * (h @ wu)) @ wd

def _rel_bucket(n):
    max_exact = NUM_BUCKETS // 2
    nf = jnp.maximum(n, 1).astype(jnp.float32)
    large = max_exact + (jnp.log(nf / max_exact) / math.log(MAX_DISTANCE / max_exact)
                         * (NUM_BUCKETS - max_exact)).astype(jnp.int32)
    large = jnp.minimum(large, NUM_BUCKETS - 1)
    return jnp.where(n < max_exact, n, large)

def _short_conv(bg, cg, xin, prev, conv_w_l):
    u = cg * xin
    T = u.shape[1]
    u_ext = jnp.concatenate([prev.astype(u.dtype), u], axis=1)
    out = sum(conv_w_l[j] * u_ext[:, j:j + T] for j in range(CONV_WIDTH))
    return bg * out, u_ext[:, -(CONV_WIDTH - 1):]

def _multi_pool(u, prev, pos0, pool_w_l, pool_scale_l):
    B, T, _ = u.shape
    u_ext = jnp.concatenate([prev.astype(u.dtype), u], axis=1)
    cs = jnp.cumsum(u_ext.astype(jnp.float32), axis=1)
    cs = jnp.pad(cs, ((0, 0), (1, 0), (0, 0)))
    end = cs[:, POOL_PREV + 1:]
    pos = pos0 + jnp.arange(T, dtype=jnp.int32)
    means = []
    for g, w in enumerate(POOL_WINDOWS):
        sl = slice(g * POOL_GROUP, (g + 1) * POOL_GROUP)
        start = cs[:, POOL_PREV + 1 - w:POOL_PREV + 1 - w + T, sl]
        cnt = jnp.minimum(w, pos + 1).astype(jnp.float32)[None, :, None]
        means.append((end[..., sl] - start) / cnt)
    mean = jnp.concatenate(means, axis=-1)
    d = (mean - u.astype(jnp.float32)).astype(u.dtype).reshape(B, T, len(POOL_WINDOWS), POOL_GROUP)
    y = jnp.einsum('btgc,gcd->btgd', d, pool_w_l).reshape(B, T, W_POOL) * pool_scale_l
    return y, u_ext[:, -POOL_PREV:]

def _index_scores(qi, wi, kidx):
    s = jax.nn.relu(jnp.einsum('bqhd,bsd->bqhs', qi, kidx).astype(jnp.float32) * IDX_DIM ** -0.5)
    return jnp.einsum('bqh,bqhs->bqs', wi.astype(jnp.float32) * IDX_HEADS ** -0.5, s)

def _sparse_attend(q, k_sel, v_sel, idx, qpos, rel_bias):
    dist = qpos[None, :, None] - idx
    valid = dist >= 0
    bias = rel_bias.astype(jnp.float32)[_rel_bucket(jnp.maximum(dist, 0))]
    logits = jnp.einsum('bqhd,bqkhd->bqhk', q, k_sel).astype(jnp.float32) * HEAD_DIM ** -0.5
    logits = logits + jnp.moveaxis(bias, -1, -2)
    logits = jnp.where(valid[:, :, None, :], logits, -jnp.inf)
    p = jax.nn.softmax(logits, axis=-1)
    return jnp.einsum('bqhk,bqkhd->bqhd', p.astype(v_sel.dtype), v_sel)

def _attn_prompt(q, k, v, qi, wi, kidx, rel_bias):
    B, S = q.shape[:2]
    top_k = min(TOPK_MAX, S // 4)
    nb = S // Q_BLOCK

    def blocks(a):
        return jnp.moveaxis(a.reshape((B, nb, Q_BLOCK) + a.shape[2:]), 1, 0)

    qpos = jnp.arange(S, dtype=jnp.int32).reshape(nb, Q_BLOCK)
    kpos = jnp.arange(S, dtype=jnp.int32)
    bidx = jnp.arange(B)[:, None, None]

    def body(args):
        q_b, qi_b, wi_b, qp = args
        sc = _index_scores(qi_b, wi_b, kidx)
        sc = jnp.where(kpos[None, None, :] <= qp[None, :, None], sc, -jnp.inf)
        _, idx = lax.top_k(sc, top_k)
        return _sparse_attend(q_b, k[bidx, idx], v[bidx, idx], idx, qp, rel_bias)

    o = lax.map(body, (blocks(q), blocks(qi), blocks(wi), qpos))
    return jnp.moveaxis(o, 0, 1).reshape(B, S, W_ATTN)

def _attn_sample(q, k_new, v_new, qi, wi, kidx_new, cache_k, cache_v, cache_kidx, layer, page_table, rel_bias):
    Bd, T = q.shape[:2]
    past = page_table.shape[1] * PAGE_SIZE
    L = past + T
    top_k = min(TOPK_MAX, L // 4)
    kidx_past = cache_kidx[layer, page_table].reshape(Bd, past, IDX_DIM)
    kidx_all = jnp.concatenate([kidx_past.astype(kidx_new.dtype), kidx_new], axis=1)
    qpos = past + jnp.arange(T, dtype=jnp.int32)
    sc = _index_scores(qi, wi, kidx_all)
    sc = jnp.where(jnp.arange(L, dtype=jnp.int32)[None, None, :] <= qpos[None, :, None], sc, -jnp.inf)
    _, idx = lax.top_k(sc, top_k)
    bidx = jnp.arange(Bd)[:, None, None]
    in_past = (idx < past)[..., None, None]
    pidx = jnp.minimum(idx, past - 1)
    phys = page_table[bidx, pidx // PAGE_SIZE]
    off = pidx % PAGE_SIZE
    nidx = jnp.clip(idx - past, 0, T - 1)
    k_sel = jnp.where(in_past, cache_k[layer, phys, off].astype(k_new.dtype), k_new[bidx, nidx])
    v_sel = jnp.where(in_past, cache_v[layer, phys, off].astype(v_new.dtype), v_new[bidx, nidx])
    return _sparse_attend(q, k_sel, v_sel, idx, qpos, rel_bias).reshape(Bd, T, W_ATTN)

def _mix(h, w_in_l, conv_w_l, pool_w_l, pool_scale_l, w_o_l, conv_prev, pool_prev, pos0, attn_fn):
    B, T, _ = h.shape
    z = h @ w_in_l
    pts, acc = [], 0
    for s in SPLITS[:-1]:
        acc += s
        pts.append(acc)
    bg, cg, xin, u, q, k, v, qi, ki, wi = jnp.split(z, pts, axis=-1)
    y_conv, conv_new = _short_conv(bg, cg, xin, conv_prev, conv_w_l)
    y_pool, pool_new = _multi_pool(u, pool_prev, pos0, pool_w_l, pool_scale_l)
    q = q.reshape(B, T, N_HEADS, HEAD_DIM)
    k = k.reshape(B, T, N_HEADS, HEAD_DIM)
    v = v.reshape(B, T, N_HEADS, HEAD_DIM)
    qi = qi.reshape(B, T, IDX_HEADS, IDX_DIM)
    y_attn = attn_fn(q, k, v, qi, wi, ki)
    out = jnp.concatenate([y_conv, y_pool, y_attn], axis=-1) @ w_o_l
    return out, conv_new, pool_new, k, v, ki

def setup_inputs(seed: int = 0) -> dict:
    key = jax.random.key(seed)
    ks = jax.random.split(key, 32)
    n_pages = PAST_LEN // PAGE_SIZE
    n_used = DEC_BATCH * n_pages
    n_phys = n_used + max(1, n_used // 4)
    f32 = jnp.float32

    def nrm(k, shape, scale=1.0):
        return jax.random.normal(k, shape, f32) * scale

    def gain(k, shape):
        return 1.0 + 0.01 * jax.random.normal(k, shape, f32)

    page_table = jax.random.permutation(ks[7], n_phys)[:n_used].reshape(DEC_BATCH, n_pages).astype(jnp.int32)
    return {
        'x_prompt': nrm(ks[0], (BATCH, SEQ, D_MODEL)),
        'x_sample': nrm(ks[1], (DEC_BATCH, DEC_SEQ, D_MODEL)),
        'cache_k': nrm(ks[2], (DEPTH, n_phys, PAGE_SIZE, N_HEADS, HEAD_DIM)),
        'cache_v': nrm(ks[3], (DEPTH, n_phys, PAGE_SIZE, N_HEADS, HEAD_DIM)),
        'cache_kidx': nrm(ks[4], (DEPTH, n_phys, PAGE_SIZE, IDX_DIM)),
        'state_conv': nrm(ks[5], (DEPTH, DEC_BATCH, CONV_WIDTH - 1, W_CONV)),
        'state_pool': nrm(ks[6], (DEPTH, DEC_BATCH, POOL_PREV, W_POOL)),
        'page_table': page_table,
        'norm_ffn1': gain(ks[8], (DEPTH, D_MODEL)),
        'ffn1_gate': nrm(ks[9], (DEPTH, D_MODEL, D_FF), D_MODEL ** -0.5),
        'ffn1_up': nrm(ks[10], (DEPTH, D_MODEL, D_FF), D_MODEL ** -0.5),
        'ffn1_down': nrm(ks[11], (DEPTH, D_FF, D_MODEL), D_FF ** -0.5),
        'norm_mix': gain(ks[12], (DEPTH, D_MODEL)),
        'w_in': nrm(ks[13], (DEPTH, D_MODEL, D_IN), D_MODEL ** -0.5),
        'conv_w': nrm(ks[14], (DEPTH, CONV_WIDTH, W_CONV), 0.5),
        'pool_w': nrm(ks[15], (DEPTH, len(POOL_WINDOWS), POOL_GROUP, POOL_GROUP), POOL_GROUP ** -0.5),
        'pool_scale': gain(ks[16], (DEPTH, W_POOL)),
        'w_o': nrm(ks[17], (DEPTH, D_MODEL, D_MODEL), D_MODEL ** -0.5),
        'norm_ffn2': gain(ks[18], (DEPTH, D_MODEL)),
        'ffn2_gate': nrm(ks[19], (DEPTH, D_MODEL, D_FF), D_MODEL ** -0.5),
        'ffn2_up': nrm(ks[20], (DEPTH, D_MODEL, D_FF), D_MODEL ** -0.5),
        'ffn2_down': nrm(ks[21], (DEPTH, D_FF, D_MODEL), D_FF ** -0.5),
        'rel_bias': nrm(ks[22], (NUM_BUCKETS, N_HEADS), 0.5),
        'norm_final': gain(ks[23], (D_MODEL,)),
    }

def reference(x_prompt, x_sample, cache_k, cache_v, cache_kidx, state_conv, state_pool, page_table,
              norm_ffn1, ffn1_gate, ffn1_up, ffn1_down, norm_mix, w_in, conv_w, pool_w, pool_scale, w_o,
              norm_ffn2, ffn2_gate, ffn2_up, ffn2_down, rel_bias, norm_final):
    xp, xs = x_prompt, x_sample
    B = xp.shape[0]
    past = page_table.shape[1] * PAGE_SIZE
    kp_l, vp_l, ip_l, cp_l, pp_l = [], [], [], [], []
    ks_l, vs_l, is_l, cs_l, ps_l = [], [], [], [], []
    for l in range(DEPTH):
        xp = xp + 0.5 * _swiglu(_rmsnorm(xp, norm_ffn1[l]), ffn1_gate[l], ffn1_up[l], ffn1_down[l])
        xs = xs + 0.5 * _swiglu(_rmsnorm(xs, norm_ffn1[l]), ffn1_gate[l], ffn1_up[l], ffn1_down[l])

        attn_p = lambda q, k, v, qi, wi, ki: _attn_prompt(q, k, v, qi, wi, ki, rel_bias)
        out_p, conv_p, pool_p, k_p, v_p, i_p = _mix(
            _rmsnorm(xp, norm_mix[l]), w_in[l], conv_w[l], pool_w[l], pool_scale[l], w_o[l],
            jnp.zeros((B, CONV_WIDTH - 1, W_CONV), xp.dtype), jnp.zeros((B, POOL_PREV, W_POOL), xp.dtype),
            0, attn_p)
        xp = xp + out_p

        attn_s = lambda q, k, v, qi, wi, ki, layer=l: _attn_sample(
            q, k, v, qi, wi, ki, cache_k, cache_v, cache_kidx, layer, page_table, rel_bias)
        out_s, conv_s, pool_s, k_s, v_s, i_s = _mix(
            _rmsnorm(xs, norm_mix[l]), w_in[l], conv_w[l], pool_w[l], pool_scale[l], w_o[l],
            state_conv[l], state_pool[l], past, attn_s)
        xs = xs + out_s

        xp = xp + 0.5 * _swiglu(_rmsnorm(xp, norm_ffn2[l]), ffn2_gate[l], ffn2_up[l], ffn2_down[l])
        xs = xs + 0.5 * _swiglu(_rmsnorm(xs, norm_ffn2[l]), ffn2_gate[l], ffn2_up[l], ffn2_down[l])

        kp_l.append(k_p); vp_l.append(v_p); ip_l.append(i_p); cp_l.append(conv_p); pp_l.append(pool_p)
        ks_l.append(k_s); vs_l.append(v_s); is_l.append(i_s); cs_l.append(conv_s); ps_l.append(pool_s)

    y_prompt = _rmsnorm(xp, norm_final)
    y_sample = _rmsnorm(xs, norm_final)
    return (y_prompt, y_sample,
            jnp.stack(kp_l), jnp.stack(vp_l), jnp.stack(ip_l), jnp.stack(cp_l), jnp.stack(pp_l),
            jnp.stack(ks_l), jnp.stack(vs_l), jnp.stack(is_l), jnp.stack(cs_l), jnp.stack(ps_l))


_drawn_inputs = setup_inputs


def setup_inputs(seed=0):
    import zlib

    import numpy as np

    out = dict(_drawn_inputs(seed))
    spreads = {}
    factors = {'norm_ffn1': 4.194,
     'norm_mix': 2.67,
     'pool_scale': 8.0,
     'norm_ffn2': 8.0,
     'norm_final': 5.796}
    for name, (base, spread) in spreads.items():
        noise = np.random.default_rng([zlib.crc32(name.encode()), seed]).standard_normal(out[name].shape)
        drawn = base * np.exp(spread * noise) if base else spread * noise
        out[name] = __import__('jax').numpy.asarray(drawn.astype(out[name].dtype))
    for name, factor in factors.items():
        out[name] = (out[name] * factor).astype(out[name].dtype)
    return out
```

```python
from contextlib import ExitStack

import numpy as np
import concourse.bass as bass
from concourse import mybir

F32 = mybir.dt.float32
F32R = mybir.dt.float32r
I32 = mybir.dt.int32
ACT = mybir.ActivationFunctionType
ALU = mybir.AluOpType
ds = bass.ds

P = 128
D, SEQ, DEPTH, DB, DT, PAST, PAGE = 1024, 512, 2, 8, 4, 1024, 128
DFF, NH, HD, IH, ID = 2816, 8, 64, 8, 64
WC, WP, WA = 256, 256, 512
NPG = PAST // PAGE
TOK = SEQ + DB * DT
HT = TOK // 2
KC = D // P
FB = DFF // 256
EPS = 1e-6
TOPK_P, TOPK_S = 128, 256
LS = PAST + 8
LT = LS // 3
NEG = -1e30
TAKEN = -3e38
QB = SEQ // P
POOLW = (2, 4, 8, 16)
SCALE = HD ** -0.5
C_BG, C_CG, C_XIN, C_U, C_Q, C_K, C_V, C_QI, C_KI, D_IN = 0, 256, 512, 768, 1024, 1536, 2048, 2560, 3072, 3144
RAW_SLOTS, SPLIT_SLOTS = 3, 6

_CW = dict(ident=128, ones=128, causal=128, causal_new=8, row_of=256, head_of=128, own_query=64, own_batch=64,
           rwin=2, rcnt=32)
CO, _n = {}, 0
for _k, _w in _CW.items():
    CO[_k] = _n
    _n += _w
NCONST = _n
NTD, NTP = LS + DT - 1, SEQ + P - 1


def shape_constants():
    c = np.zeros((P, NCONST), np.float32)
    p = np.arange(P)
    c[:, CO['ident']:CO['ident'] + P] = np.eye(P)
    c[:, CO['ones']:CO['ones'] + P] = 1.0
    c[:, CO['causal']:CO['causal'] + P] = np.where(p[None, :] <= p[:, None], 0.0, NEG)
    j = np.arange(8)
    c[:DB * DT, CO['causal_new']:CO['causal_new'] + 8] = np.where(
        (j[None, :] <= np.arange(DB * DT)[:, None] % DT) & (j[None, :] < DT), 0.0, NEG)
    pb, ph, pt = p // 32, p % 32 // 4, p % 4
    bt = np.arange(32)
    for g in range(2):
        own_b = bt[:, None] // 4 == 4 * g + pb[None, :]
        own_bt = own_b & (bt[:, None] % 4 == pt[None, :])
        c[:32, CO['row_of'] + g * P:CO['row_of'] + (g + 1) * P] = own_bt
        c[:, CO['own_query'] + 32 * g:CO['own_query'] + 32 * g + 32] = own_bt.T * IH ** -0.5
        c[:, CO['own_batch'] + 32 * g:CO['own_batch'] + 32 * g + 32] = own_b.T
    c[P - IH:, CO['head_of']:CO['head_of'] + P] = np.arange(IH)[:, None] == ph[None, :]
    for jc in range(2):
        for half in range(2):
            w = POOLW[2 * jc + half]
            r = slice(64 * half, 64 * half + 64)
            c[r, CO['rwin'] + jc] = 1.0 / w
            c[r, CO['rcnt'] + 16 * jc:CO['rcnt'] + 16 * jc + 16] = 1.0 / np.minimum(w, np.arange(16) + 1)
    return c


def bucket_one_hots():
    dist = np.concatenate([PAST + DT - 1 - np.arange(NTD), SEQ - 1 - np.arange(NTP)])
    n = np.maximum(dist, 0)
    nf = np.maximum(n, 1).astype(np.float32)
    large = 16 + (np.log(nf / 16) / np.float32(np.log(8.0)) * 16).astype(np.int32)
    b = np.where(n < 16, n, np.minimum(large, 31))
    return (np.arange(32)[:, None] == b[None, :]).astype(np.float32)


Z_TILES = ['KI', 'WI', 'QI0', 'QI1', 'QI2', 'QI3',
           'CG0', 'XIN0', 'BG0', 'U0', 'Q0', 'Q1', 'Q2', 'Q3', 'K0', 'K1', 'K2', 'K3',
           'V0', 'V1', 'V2', 'V3', 'CG1', 'XIN1', 'BG1', 'U1']
Z_NO = {n: i for i, n in enumerate(Z_TILES)}
MIX = ['STATS', 'ST'] + Z_TILES[:6] + ['WT'] + [f'IS{n}' for n in range(12)]
MIX += [f'KIT{b}' for b in range(DB)] + ['SC'] + Z_TILES[6:18] + ['TL0', 'PM0'] + Z_TILES[18:22]
MIX += ['KIN'] + [f'NT{n}' for n in range(5)] + Z_TILES[22:]
for _b in range(DB):
    MIX += [f'KT{_b}_0', f'KT{_b}_1'] + ['TL1', 'PM1'] * (_b == 4) + [f'KT{_b}_2', f'KT{_b}_3']
MIX += ['MX0', 'MX1', 'PTR0', 'PTN0', 'PTR1', 'PTN1']
for _n in range(18):
    MIX += [f'PL{_n}'] * (_n < 16) + [f'PT{_n - 1}'] * (1 <= _n < 17) + [f'PO{_n - 2}'] * (_n >= 2)
MIX += [f'WO{n}' for n in range(8)]
MIX_NO = {n: i for i, n in enumerate(MIX)}
assert len(MIX_NO) == len(MIX)

T_FFN = 1 + 4 + 12 * (FB - 1) + 8
T_MIX = len(MIX)
T_LAYER = 2 * T_FFN + T_MIX
T_START = 5 + 3
U_FFN, U_MIX = 6 * FB, 36
U_LAYER = 2 * U_FFN + U_MIX
X_LAYER = 8 * FB * 2 + 8
X_START = 5
TOPK_STEPS = 16 * 6 + 32 * 2
POOL_CHAIN = 43
OUT_SMALL = 10
S_IN = 4 + 5 * DEPTH


def trunk(nc, a):
    ctx = ExitStack()
    with ctx:
        sem_n = [0]

        def sem(name):
            sem_n[0] += 1
            return ctx.enter_context(nc.semaphore(name))

        base = 16512
        place = [base]

        def region(nbytes):
            at = place[0]
            place[0] += (nbytes + 31) // 32 * 32
            assert place[0] <= 229368, place[0]
            return at

        def at(name, shape, offset, dt=F32):
            return nc.alloc_sbuf_tensor_at(name, shape, dt, offset=offset)

        r_x, r_hhi, r_hlo = region(KC * TOK * 4), region(KC * TOK * 4), region(KC * TOK * 4)
        xT = at("xT", [P, KC, TOK], r_x)
        h_hi = at("h_hi", [P, KC, TOK], r_hhi, F32R)
        h_lo = at("h_lo", [P, KC, TOK], r_hlo, F32R)
        sq = at("sq", [P, KC, TOK], r_hlo)
        kpages = at("kpages", [P, NPG, WA], r_hhi)
        keysT = at("keysT", [P, 4, LS], r_hlo)
        strip = at("strip", [P, NH, SEQ], r_hhi)
        r_cat = region(KC * TOK * 4)
        cat = at("cat", [P, KC, TOK], r_cat)
        act_hi = at("act_hi", [P, 2, TOK], r_cat, F32R)
        act_lo = at("act_lo", [P, 2, TOK], r_cat + 2 * TOK * 4, F32R)
        srelu = at("srelu", [P, 2, 3, LT], r_cat + 4 * TOK * 4)
        yst = at("yst", [P, 2, D], r_cat)
        r_sg = region(4 * TOK * 4)
        silu = at("silu", [P, 2, TOK], r_sg)
        gated = at("gated", [P, 2, TOK], r_sg + 2 * TOK * 4)
        normed = at("normed", [P, 2, TOK], r_sg)
        prelu = at("prelu", [P, 2, 2, SEQ], r_sg)
        kn_stage = at("kn_stage", [P, 2, WA], r_sg)
        probs = at("probs", [P, 2, 2, SEQ], r_sg)
        r_raw = region(RAW_SLOTS * 4096)
        raw = at("raw", [P, RAW_SLOTS, 1024], r_raw)
        lg = at("lg", [P, 2, LS], r_raw)
        r_whi, r_wlo = region(SPLIT_SLOTS * 4096), region(SPLIT_SLOTS * 4096)
        w_hi = at("w_hi", [P, SPLIT_SLOTS, 1024], r_whi, F32R)
        w_lo = at("w_lo", [P, SPLIT_SLOTS, 1024], r_wlo, F32R)
        vpages = [at("vpages0", [P, NPG, WA], r_whi), at("vpages1", [P, NPG, WA], r_wlo)]
        pTs = at("pTs", [P, NPG, P], r_whi + 16384)
        pTn = at("pTn", [32, P], r_whi + 20480)
        pnew = at("pnew", [P, 32], r_whi + 20992)
        pTp = at("pTp", [P, 2, SEQ], r_wlo + 16384)
        oh = at("oh", [32, NTD + NTP], r_whi)
        r_qk, r_q, r_cz = region(4 * TOK * 4), region(4 * TOK * 4), region(4 * TOK * 4)
        qi = at("qi", [P, 4, TOK], r_qk)
        kT = at("kT", [P, 4, TOK], r_qk)
        qT = at("qT", [P, 4, TOK], r_q)
        kidxT = at("kidxT", [ID, 2, LS], r_q)
        cz = at("cz", [P, 4, TOK], r_cz)
        ki = at("ki", [P, TOK], region(TOK * 4))
        wi = at("wi", [P, TOK], region(TOK * 4))
        NUX = 2 + SEQ + DB * 6
        ucx = at("ucx", [P, NUX], region(NUX * 4))
        NPX = 15 + SEQ + DB * 19
        r_pb = region(3 * 2720)
        pb = [at(f"pb{n}", [P, NPX], r_pb + 2720 * n) for n in range(3)]
        tp_sb = at("tp_sb", [NH, NTP], r_pb + 2720)
        conv_t = [at(f"conv_t{n}", [P, NUX], r_pb + 2720 * (1 + n)) for n in range(2)]
        qz = at("qz", [P, 4, DB, 32], r_cat + 4 * TOK * 4)
        work_p = at("work_p", [P, P * (2 + 3 + 4)], region(P * 9 * 4))
        work_s = at("work_s", [32, LS], region(LS * 4))
        r_vn = region(5 * WA * 4)
        vn = at("vn", [P, 5, WA], r_vn)
        kipages = at("kipages", [P, 2, NPG, ID], r_vn)
        bias_s = at("bias_s", [P, LS], region(LS * 4))
        cst = at("cst", [P, NCONST], region(NCONST * 4))
        rstd = at("rstd", [P, TOK], r_pb)
        vecs = at("vecs", [P, DEPTH * 32 + 8], region((DEPTH * 32 + 8) * 4))
        lv = at("lv", [P, 32], region(128))
        states = at("states", [P, 2, 2 * 16 // 2 + 120], region(2 * 136 * 4))
        pw = at("pw", [P, 2, P], region(1024))
        wi_nat = at("wi_nat", [P, 4, IH], region(128))
        wsel = at("wsel", [P, 2, 32], region(256))
        qis = at("qis", [ID, DB, 32], region(1024))
        top8 = at("top8", [P, 3, 8], region(96))
        stat = at("stat", [P, 2, 8], region(64))
        sstat = at("sstat", [P, 2, 4], region(32))
        rel_sb = at("rel_sb", [32, NH], region(32))
        relx = at("relx", [32, DT, P], r_wlo + 4096)
        epsb = at("epsb", [P, 1], region(32))
        pt_sb = at("pt_sb", [1, DB * NPG], region(DB * NPG * 4), I32)
        vrows = at("vrows", [P, P], r_wlo + 8192)
        srow = at("srow", [P, 2, WC], r_vn + 4096)
        tail_st = at("tail_st", [47, 2, P], r_sg + 5376)
        conv_st = at("conv_st", [6 * DB, 2, 2 * P], r_sg + 6400)
        ki_st = at("ki_st", [P, 5, ID], r_sg + 4096)

        C = lambda name, rows=P, n=None, off=0: cst[0:rows, CO[name] + off:CO[name] + off + (n or _CW[name])]
        ident = C('ident')
        halves = lambda ap: ap.rearrange("p (a b) -> p a b", a=2)
        WOFF = {1: 0, 2: 2 * P, 3: 5 * P}

        ps = ctx.enter_context(nc.psum_tensor("ps", [P, 8, 512], F32))
        pair = lambda p, rows=P, n=HT: ps[0:rows, 2 * p:2 * p + 2, 0:n]

        loaded = [sem(f"raw_loaded{r}") for r in range(RAW_SLOTS)]
        units_hi = sem("units_hi")
        units_split = sem("units_split")
        tiles = sem("tiles")
        x_updates = sem("x_updates")
        sq_done, rt_done, rstd_done = sem("sq_done"), sem("rt_done"), sem("rstd_done")
        normed_done, hhi_done, h_ready = sem("normed_done"), sem("hhi_done"), sem("h_ready")
        silu_done, gu_done = sem("silu_done"), sem("gu_done")
        acthi_done, act_ready = sem("acthi_done"), sem("act_ready")
        s_in, s_oh, s_scr = sem("start_loads"), sem("onehots_loaded"), sem("bias_scratch")
        s_xrow = [sem("xrow0"), sem("xrow1")]
        zeroed, relx_done, tp_done = sem("zeroed"), sem("relx_done"), sem("tp_done")
        lv_done, st_loaded, pw_loaded, st_done = sem("lv_done"), sem("st_loaded"), sem("pw_loaded"), sem("st_done")
        z_done, wt_done, relu_done, iacc_done = sem("z_done"), sem("wt_done"), sem("relu_done"), sem("iacc_done")
        kidx_loaded = [sem("kidx_loaded0"), sem("kidx_loaded1")]
        kit_done, score_mm, srelu_done, sc_done = sem("kit_done"), sem("score_mm"), sem("srelu_done"), sem("sc_done")
        topk, masks_done = sem("topk_steps"), sem("masks_done")
        pool_chain = sem("pool_chain")
        ucx_done, d_done, qz_done = sem("ucx_done"), sem("d_done"), sem("qz_done")
        keys_padded = sem("keys_padded")
        tail_done, pm_done, kin_done, nat_done = sem("tail_done"), sem("pm_done"), sem("kin_done"), sem("nat_done")
        k_loaded = [sem("k_loaded0"), sem("k_loaded1")]
        v_loaded = [sem("v_loaded0"), sem("v_loaded1")]
        keys_done, logit_mm, lg_done, lgb_done = sem("keys_done"), sem("logit_mm"), sem("lg_done"), sem("lgb_done")
        slog_done, sexp_done, snorm_done = sem("slog_done"), sem("sexp_done"), sem("snorm_done")
        ptr_done, sout_mm, sout_done = sem("ptr_done"), sem("sout_mm"), sem("sout_done")
        strip_loaded = sem("strip_loaded")
        plog_done, pexp_done, pnorm_done = sem("plog_done"), sem("pexp_done"), sem("pnorm_done")
        ppt_done, po_done = sem("ppt_done"), sem("po_done")
        cathi_done, cat_ready = sem("cathi_done"), sem("cat_ready")
        out_nat = [sem("out_nat0"), sem("out_nat1")]
        out_small, y_done = sem("out_small"), sem("y_done")
        s_y = [sem("out_y0"), sem("out_y1")]
        passed = {n: sem(f"passed_{n}") for n in ("sp", "act", "pool", "dve", "pe")}

        def hold(eng, who, s, v):
            eng.wait_ge(s, v)
            eng.sem_inc(passed[who], 1)

        def unit0(l, ph):
            return l * U_LAYER + (0, U_FFN, U_FFN + U_MIX)[ph]

        def tile0(l, ph):
            return l * T_LAYER + T_START + (0, T_FFN, T_FFN + T_MIX)[ph]

        def x0(l, ph):
            return l * X_LAYER + X_START + (0, 8 * FB, 8 * FB + 8)[ph]

        def T(l, name):
            return tile0(l, 1) + MIX_NO[name] + 1

        def norm_no(l, ph):
            return l * 3 + ph

        TAIL = SEQ - 15
        NEWROWS = DB * DT
        rows_of = lambda t: P if t < 4 else NEWROWS
        CONV_TAPS, POOL_SC = 24, 30

        block = ctx.enter_context(nc.Block())

        @block.sync
        def _(sp):
            def load(l, ph, i, c, dst, src):
                hold(sp, "sp", units_split, unit0(l, ph) + 6 * i + c + 1)
                sp.dma_start(dst, src).then_inc(loaded[c % 3], 16)

            def k_rows(c):
                return raw[:, c % 3, :].rearrange("p (k n) -> p k n", k=KC)

            def ffn(l, f):
                ph = 2 * f
                gate, up = (a[f'ffn{f + 1}_{n}'].rearrange("l (k p) f -> l p k f", p=P) for n in ('gate', 'up'))
                down = a[f'ffn{f + 1}_down']

                def gate_up(i, j, c0):
                    for n, w in enumerate((gate, gate, up, up)):
                        load(l, ph, j, c0 + n, k_rows(c0 + n), w[l, :, :, ds(i * 256 + P * (n % 2), P)])

                def down_rows(i, j, c0):
                    for m in range(2):
                        load(l, ph, j, c0 + m, raw[:, (c0 + m) % 3, :], down[l, ds(i * 256 + m * P, P), :])

                gate_up(0, 0, 0)
                with sp.Fori(0, FB - 1) as j:
                    gate_up(j + 1, j, 4)
                    down_rows(j, j, 8)
                down_rows(FB - 1, 0, U_FFN - 2)

            sp.dma_start(cst[:, :], a['consts']).then_inc(s_in, 16)
            sp.dma_start(rel_sb[:, :], a['rel_bias']).then_inc(s_in, 16)
            sp.dma_start(pt_sb[0:1, :], a['page_table'].rearrange("(o b) n -> o (b n)", o=1)).then_inc(s_in, 16)
            for l in range(DEPTH):
                for n, v in enumerate(('norm_ffn1', 'norm_mix', 'norm_ffn2')):
                    sp.dma_start(vrows[l * 32 + 8 * n:l * 32 + 8 * n + 8, :],
                                 a[v][l, :].rearrange("(c p) -> c p", p=P)).then_inc(s_in, 16)
                sp.dma_start(vrows[l * 32 + 24:l * 32 + 30, :],
                             a['conv_w'][l, :, :].rearrange("j (c p) -> (j c) p", p=P)).then_inc(s_in, 16)
                sp.dma_start(vrows[l * 32 + 30:l * 32 + 32, :],
                             a['pool_scale'][l, :].rearrange("(c p) -> c p", p=P)).then_inc(s_in, 16)
            sp.dma_start(vrows[DEPTH * 32:DEPTH * 32 + 8, :],
                         a['norm_final'].rearrange("(c p) -> c p", p=P)).then_inc(s_in, 16)
            sp.dma_start(oh[:, :], a['onehots']).then_inc(s_oh, 16)
            sp.dma_start(a['pool_sample'].rearrange("l b t c -> (l b) t c")[:, 0:11, :],
                         a['state_pool'].rearrange("l b t c -> (l b) t c")[:, DT:15, :]).then_inc(out_small, 16)
            for t in range(5):
                if t >= 2:
                    sp.wait_ge(tiles, t - 1)
                src = (a['x_prompt'][0, t * P:(t + 1) * P, :] if t < 4
                       else a['x_sample'].rearrange("b t d -> (b t) d"))
                sp.dma_start(yst[0:rows_of(t), t % 2, :], src).then_inc(s_xrow[t % 2], 16)
            sp.wait_ge(tp_done, 2)
            sp.dma_start(a['scratch'], tp_sb[:, :].unsqueeze(1).to_broadcast([NH, P, NTP])).then_inc(s_scr, 16)

            w_in = a['w_in'].rearrange("l (k p) f -> l p k f", p=P)
            w_o = a['w_o'].rearrange("l (k p) f -> l p k f", p=P)
            ck, cv = (a[n].rearrange("l n p h d -> l n p (h d)") for n in ('cache_k', 'cache_v'))
            last_page = a['cache_k'].shape[1] - 1
            first_col = dict(QI=C_QI, CG=C_CG, XIN=C_XIN, BG=C_BG, U=C_U, Q=C_Q, K=C_K, V=C_V)

            def pages(l, b, pg0, n, dst, src, s):
                for pg in range(pg0, pg0 + n):
                    at_ = b * NPG + pg
                    page = sp.value_load(pt_sb[0:1, at_:at_ + 1], min_val=0, max_val=last_page)
                    sp.dma_start(dst[:, pg, :], src[l, page, :, :]).then_inc(s, 16)

            with sp.Fori(0, DEPTH) as l:
                ffn(l, 0)

                hold(sp, "sp", tiles, tile0(l, 0) + 1)
                sp.dma_start(srow[0:DB * 15, 0, :], a['state_pool'].rearrange("l b t c -> l (b t) c")[l, :, :]).then_inc(st_loaded, 16)
                sp.dma_start(srow[0:DB * 2, 1, :], a['state_conv'].rearrange("l b t c -> l (b t) c")[l, :, :]).then_inc(st_loaded, 16)
                for g in range(4):
                    r = 64 * (g % 2)
                    sp.dma_start(pw[r:r + 64, g // 2, r:r + 64], a['pool_w'][l, g, :, :]).then_inc(pw_loaded, 16)
                for c in range(4):
                    k0, s = 4 * (c % 2), raw[:, c % 3, 0:512].rearrange("p (k n) -> p k n", k=4)
                    if c < 2:
                        load(l, 1, 0, c, s[:, :, 0:ID], w_in[l, :, k0:k0 + 4, C_KI:C_KI + ID])
                        sp.dma_start(s[:, :, ID:2 * ID], w_in[l, :, k0:k0 + 4, C_KI:C_KI + ID]).then_inc(loaded[c % 3], 16)
                    else:
                        load(l, 1, 0, c, s, w_in[l, :, k0:k0 + 4, D_IN - P:D_IN])

                def z_unit(n):
                    f0 = first_col[Z_TILES[n][:-1]] + P * int(Z_TILES[n][-1])
                    load(l, 1, 0, n + 2, k_rows(n + 2), w_in[l, :, :, f0:f0 + P])

                for n in range(2, 6):
                    z_unit(n)
                for b in range(2):
                    pages(l, b, 0, NPG, kipages[:, b % 2], a['cache_kidx'], kidx_loaded[b % 2])
                for n in range(6, 9):
                    z_unit(n)
                for b in range(2, DB):
                    hold(sp, "sp", tiles, T(l, f'KIT{b - 2}'))
                    pages(l, b, 0, NPG, kipages[:, b % 2], a['cache_kidx'], kidx_loaded[b % 2])
                for n in range(9, 26):
                    z_unit(n)

                def keys(b):
                    for hf in range(2):
                        hold(sp, "sp", tiles, T(l, f'KT{b - 1}_{2 * hf + 1}' if b else 'U1'))
                        pages(l, b, 4 * hf, 4, kpages, ck, k_loaded[hf])

                hold(sp, "sp", kin_done, l * 2 + 2)
                sp.dma_start(a['kidx_prompt'].rearrange("l b (t p) d -> l p (b t) d", p=P)[l, :, :, :], ki_st[:, 0:4, :]).then_inc(out_small, 16)
                sp.dma_start(a['kidx_sample'].rearrange("l b t d -> l (b t) d")[l, :, :], ki_st[0:NEWROWS, 4, :]).then_inc(out_small, 16)
                for t in range(5):
                    hold(sp, "sp", nat_done, l * 10 + 2 * t + 2)
                    for n, rows in (('k', kn_stage[0:rows_of(t), t % 2, :]), ('v', vn[0:rows_of(t), t, :])):
                        dst = (a[n + '_prompt'].rearrange("l b s h d -> l (b s) (h d)")[l, t * P:(t + 1) * P, :] if t < 4
                               else a[n + '_sample'].rearrange("l b s h d -> l (b s) (h d)")[l, :, :])
                        sp.dma_start(dst, rows).then_inc(out_nat[t % 2], 16)
                keys(0)
                for b in range(2):
                    pages(l, b, 0, NPG, vpages[b], cv, v_loaded[b])
                for b in range(1, 5):
                    keys(b)
                hold(sp, "sp", tail_done, l * 6 + 6)
                sp.dma_start(a['pool_prompt'].rearrange("l b t (j c) -> l (b t) j c", c=P)[l, :, :, :], tail_st[0:15, :, :]).then_inc(out_small, 16)
                for t in range(DT):
                    sp.dma_start(a['pool_sample'].rearrange("l b t (j c) -> l b t j c", c=P)[l, :, 11 + t, :, :],
                                 tail_st[15 + t:15 + t + 4 * DB - 3:4, :, :]).then_inc(out_small, 16)
                for t in range(2):
                    sp.dma_start(a['conv_sample'].rearrange("l b t (j c) -> l b t j c", c=P)[l, :, t, :, :],
                                 conv_st[4 + t:4 + t + 6 * DB - 5:6, :, 0:P]).then_inc(out_small, 16)
                sp.dma_start(a['conv_prompt'].rearrange("l b t (j c) -> l (b t) j c", c=P)[l, :, :, :], conv_st[0:2, :, P:2 * P]).then_inc(out_small, 16)
                for b in range(5, DB):
                    keys(b)
                hold(sp, "sp", s_scr, 16)
                hold(sp, "sp", tiles, T(l, f'KT{DB - 1}_3'))
                for h in range(NH):
                    src = bass.AP(a['scratch'].tensor, h * P * NTP + P - 1, [[NTP - 1, P], [1, SEQ]])
                    sp.dma_start(strip[:, h, :], src).then_inc(strip_loaded, 16)
                for b in range(2, DB):
                    hold(sp, "sp", sout_mm, l * DB + b - 1)
                    pages(l, b, 0, NPG, vpages[b % 2], cv, v_loaded[b % 2])
                hold(sp, "sp", tiles, T(l, 'PO15'))
                for n in range(8):
                    load(l, 1, 0, 28 + n, k_rows(28 + n), w_o[l, :, :, n * P:(n + 1) * P])
                ffn(l, 1)

            for t in range(5):
                sp.wait_ge(y_done, t + 1)
                dst = (a['y_prompt'][0, t * P:(t + 1) * P, :] if t < 4 else a['y_sample'].rearrange("b t d -> (b t) d"))
                sp.dma_start(dst, yst[0:rows_of(t), t % 2, :]).then_inc(s_y[t % 2], 16)
            sp.wait_ge(s_y[0], 48)
            sp.wait_ge(s_y[1], 32)
            sp.wait_ge(out_nat[0], DEPTH * 96)
            sp.wait_ge(out_nat[1], DEPTH * 64)
            sp.wait_ge(out_small, 16 + DEPTH * 16 * OUT_SMALL)

        @block.scalar
        def _(act):
            def raw_loads(l, ph, i, c):
                twice = 16 if c % 3 < 2 else 0
                before = (0, U_FFN, U_FFN + U_MIX)[ph] // 3
                return l * (16 * (U_LAYER // 3) + twice) + 32 * i + 16 * (before + c // 3 + 1) + (twice if ph else 0)

            def hi(l, ph, i, c, n=1024, slot_free=None):
                if slot_free is not None:
                    act.wait_ge(tiles, slot_free)
                act.wait_ge(loaded[c % 3], raw_loads(l, ph, i, c))
                act.activation(w_hi[:, c % 6, 0:n], raw[:, c % 3, 0:n], ACT.Copy).then_inc(units_hi, 1)

            def norm(stats_done, xready, early):
                for c in range(KC):
                    act.wait_ge(x_updates, xready - (KC - 1 - c if early else 0))
                    act.activation(sq[:, c, :], xT[:, c, :], ACT.Square).then_inc(sq_done, 1)
                act.wait_ge(tiles, stats_done)
                act.activation(halves(rstd[:, :]), pair(0), ACT.Sqrt, scale=1.0 / D, bias=epsb[:, 0:1]).then_inc(rt_done, 1)

            def split_h(l, ph):
                for c in range(KC):
                    act.wait_ge(normed_done, norm_no(l, ph) * KC + c + 1)
                    act.activation(h_hi[:, c, :], normed[:, c % 2, :], ACT.Copy,
                                   scale=lv[:, 8 * ph + c:8 * ph + c + 1]).then_inc(hhi_done, 1)

            def ffn(l, f):
                ph = 2 * f
                t0, s0 = tile0(l, ph), (l * 2 + f) * 2 * FB
                norm(t0 + 1, x0(l, ph), early=False)
                hi(l, ph, 0, 0)
                hi(l, ph, 0, 1)
                split_h(l, ph)

                def silu_of(m, tile):
                    act.wait_ge(tiles, tile)
                    act.activation(halves(silu[:, m, :]), pair(m), ACT.Silu).then_inc(silu_done, 1)

                def act_high(i, down_done):
                    act.wait_ge(tiles, down_done)
                    for m in range(2):
                        act.wait_ge(gu_done, s0 + 2 * i + m + 1)
                        act.activation(act_hi[:, m, :], gated[:, m, :], ACT.Copy).then_inc(acthi_done, 1)

                for c in range(4):
                    hi(l, ph, 0, c + 2)
                    if c < 2:
                        silu_of(c, t0 + 2 + c)
                act_high(0, t0 + 1)
                with act.Fori(0, FB - 1) as j:
                    for c in range(4, 10):
                        hi(l, ph, j, c + 2, slot_free=t0 + 12 * j + (-4, -3, 5, 5, 6, 7)[c - 4])
                        if c < 6:
                            act.wait_ge(gu_done, s0 + 2 * j + c - 3)
                            silu_of(c - 4, t0 + 12 * j + c + 2)
                    act_high(j + 1, t0 + 12 * j + 17)

            act.wait_ge(tiles, 7)
            act.activation(tp_sb[:, 0:512], ps[0:NH, 4, :], ACT.Copy).then_inc(tp_done, 1)
            act.activation(tp_sb[:, 512:NTP], ps[0:NH, 5, 0:NTP - 512], ACT.Copy).then_inc(tp_done, 1)
            act.wait_ge(tiles, T_START)

            with act.Fori(0, DEPTH) as l:
                act.wait_ge(lv_done, l + 1)
                ffn(l, 0)
                norm(T(l, 'STATS'), x0(l, 1), early=True)
                hi(l, 1, 0, 0, 512)
                hi(l, 1, 0, 1, 512)
                act.wait_ge(tiles, T(l, 'ST'))
                act.activation(states[:, :, :], ps[:, 2:4, 0:136], ACT.Copy).then_inc(st_done, 1)
                split_h(l, 1)
                zdst = {'KI': ki[:, :], 'WI': wi[:, :]}
                for c in range(4):
                    zdst |= {f'QI{c}': qi[:, c, :], f'Q{c}': qT[:, c, :], f'K{c}': kT[:, c, :], f'V{c}': cz[:, c, :]}
                for j in range(2):
                    zdst |= {n + str(j): cz[:, q, :] for q, n in enumerate(('CG', 'XIN', 'BG', 'U'))}

                def z(name):
                    act.wait_ge(tiles, T(l, name))
                    act.activation(halves(zdst[name]), pair((Z_NO[name] + 2) % 4), ACT.Copy).then_inc(z_done, 1)

                def hi_m(c):
                    prev = c - 6
                    name = ('KI' if prev < 2 else Z_TILES[max(prev - 2, 1)] if prev < 28 else f'WO{prev - 28}')
                    hi(l, 1, 0, c, slot_free=T(l, name))

                def z_with_hi(first, last, ahead=4):
                    for n in range(first, last):
                        if n + ahead < 6:
                            hi(l, 1, 0, n + ahead)
                        else:
                            hi_m(n + ahead)
                        z(Z_TILES[n])

                hi(l, 1, 0, 2, 512)
                hi(l, 1, 0, 3, 512)
                z_with_hi(0, 6)
                for n in range(12):
                    L = (2 + n // 4) * P
                    act.wait_ge(tiles, T(l, f'IS{n}'))
                    if n >= 2:
                        act.wait_ge(iacc_done, l * 27 + 2 * (n - 1))
                    act.activation(prelu[:, n % 2, :, 0:L], pair(2 + n % 2, P, L), ACT.Relu, scale=ID ** -0.5).then_inc(relu_done, 1)
                hold(act, "act", wt_done, l * 6 + 6)
                for b in range(DB):
                    act.wait_ge(tiles, T(l, f'KIT{b}'))
                    if b >= 2:
                        hold(act, "act", score_mm, l * DB + b - 1)
                    act.activation(kidxT[:, b % 2, 0:PAST].rearrange("p (a b) -> p a b", a=2), pair(2 + b % 2, ID, 512), ACT.Copy).then_inc(kit_done, 1)
                    act.activation(kidxT[:, b % 2, PAST:PAST + DT], ki[0:ID, SEQ + DT * b:SEQ + DT * (b + 1)], ACT.Copy).then_inc(kit_done, 1)
                    if b == 4:
                        act.wait_ge(score_mm, l * DB + 4)
                        act.activation(srelu[:, 0, :, :], ps[:, 0:3, 0:LT], ACT.Relu, scale=ID ** -0.5).then_inc(srelu_done, 1)
                act.wait_ge(score_mm, l * DB + DB)
                act.activation(srelu[:, 1, :, :], ps[:, 0:3, 0:LT], ACT.Relu, scale=ID ** -0.5).then_inc(srelu_done, 1)
                act.wait_ge(tiles, T(l, 'SC'))
                act.activation(work_s[:, :].rearrange("p (a b) -> p a b", a=3), ps[0:32, 4:7, 0:LT], ACT.Copy).then_inc(sc_done, 1)

                def tail_and_pooled(j):
                    act.wait_ge(tiles, T(l, f'TL{j}'))
                    act.activation(tail_st[:, j, :], ps[0:47, 0, 0:P], ACT.Copy).then_inc(tail_done, 1)
                    act.activation(conv_st[:, j, 0:P], ps[0:6 * DB, 1, 0:P], ACT.Copy).then_inc(tail_done, 1)
                    act.activation(conv_st[0:2, j, P:2 * P], ps[0:2, 1, P:2 * P], ACT.Copy).then_inc(tail_done, 1)
                    act.wait_ge(tiles, T(l, f'PM{j}'))
                    act.activation(halves(cat[:, 2 + j, :]), pair(1), ACT.Copy, scale=lv[:, POOL_SC + j:POOL_SC + j + 1]).then_inc(pm_done, 1)

                z_with_hi(6, 18)
                hi_m(22)
                hi_m(23)
                act.wait_ge(iacc_done, l * 27 + 24)
                tail_and_pooled(0)
                for n in range(18, 22):
                    z(Z_TILES[n])
                for c in range(24, 26):
                    hi_m(c)
                act.wait_ge(tiles, T(l, 'KIN'))
                act.activation(ki_st[:, 0:4, :], ps[:, 0, 0:4 * ID].rearrange("p (t d) -> p t d", d=ID), ACT.Copy).then_inc(kin_done, 1)
                act.activation(ki_st[0:NEWROWS, 4, :], ps[0:NEWROWS, 0, 4 * ID:5 * ID], ACT.Copy).then_inc(kin_done, 1)
                for t in range(5):
                    act.wait_ge(tiles, T(l, f'NT{t}'))
                    if t >= 2:
                        act.wait_ge(out_nat[t % 2], l * (96, 64)[t % 2] + 32 * (t // 2))
                    bank = 2 * ((t + 1) % 4)
                    act.activation(kn_stage[0:rows_of(t), t % 2, :], ps[0:rows_of(t), bank, :], ACT.Copy).then_inc(nat_done, 1)
                    act.activation(vn[0:rows_of(t), t, :], ps[0:rows_of(t), bank + 1, :], ACT.Copy).then_inc(nat_done, 1)
                for n in range(22, 26):
                    if n < 24:
                        hi_m(n + 4)
                    z(Z_TILES[n])
                for b in range(DB):
                    for j in range(4):
                        act.wait_ge(tiles, T(l, f'KT{b}_{j}'))
                        if j == 0 and b > 0:
                            hold(act, "act", logit_mm, l * DB + b)
                        act.activation(keysT[:, :, 256 * j:256 * j + 256],
                                       ps[:, 4 + 2 * (j % 2):6 + 2 * (j % 2), :].rearrange("p a (c n) -> p (a c) n", n=256),
                                       ACT.Copy).then_inc(keys_done, 1)
                    act.activation(keysT[:, :, PAST:PAST + DT], kT[:, :, SEQ + DT * b:SEQ + DT * (b + 1)], ACT.Copy).then_inc(keys_done, 1)
                    if b % 4 == 3:
                        act.wait_ge(logit_mm, l * DB + b + 1)
                        act.activation(lg[:, b // 4, :].rearrange("p (a b) -> p a b", a=3), ps[:, 0:3, 0:LT], ACT.Copy, scale=SCALE).then_inc(lg_done, 1)
                    if b == 3:
                        tail_and_pooled(1)
                for g in range(2):
                    act.wait_ge(slog_done, l * 4 + 2 * g + 2)
                    act.activation(lg[:, g, :], lg[:, g, :], ACT.Exp, bias=sstat[:, g, 1:2], accum_out=sstat[:, g, 2:3]).then_inc(sexp_done, 1)

                for n in range(18):
                    if n < 16:
                        L = (n // 4 + 1) * P
                        act.wait_ge(plog_done, l * 64 + 4 * n + 4)
                        for e in range(2):
                            act.activation(probs[:, n % 2, e, 0:L], probs[:, n % 2, e, 0:L], ACT.Exp,
                                           bias=stat[:, n % 2, 2 + e:3 + e], accum_out=stat[:, n % 2, 4 + e:5 + e]).then_inc(pexp_done, 1)
                    if n >= 2:
                        m = n - 2
                        act.wait_ge(tiles, T(l, f'PO{m}'))
                        act.activation(cat[:, 4 + m % 4, P * (m // 4):P * (m // 4) + P], ps[:, 6, 0:P], ACT.Copy).then_inc(po_done, 1)
                    if 1 <= n < 17:
                        L = ((n - 1) // 4 + 1) * P
                        act.wait_ge(tiles, T(l, f'PT{n - 1}'))
                        if n >= 2:
                            act.wait_ge(tiles, T(l, f'PO{n - 2}'))
                        act.activation(pTp[:, :, 0:L], pair(2, P, L), ACT.Copy).then_inc(ppt_done, 1)

                act.wait_ge(sout_done, l * 4 + 4)
                act.wait_ge(po_done, (l + 1) * 16)
                for c in range(KC):
                    act.activation(h_hi[:, c, :], cat[:, c, :], ACT.Copy).then_inc(cathi_done, 1)
                for n in range(8):
                    hi_m(28 + n)
                ffn(l, 1)

            norm(T_START + DEPTH * T_LAYER + 1, X_START + DEPTH * X_LAYER, early=False)
            for c in range(KC):
                act.wait_ge(normed_done, 3 * DEPTH * KC + c + 1)
                act.activation(sq[:, c, :], normed[:, c % 2, :], ACT.Copy, scale=vecs[:, DEPTH * 32 + c:DEPTH * 32 + c + 1]).then_inc(hhi_done, 1)
            for t in range(5):
                act.wait_ge(tiles, T_START + DEPTH * T_LAYER + 2 + t)
                if t >= 2:
                    act.wait_ge(s_y[t % 2], 16 * (t // 2))
                b0 = 2 * (t % 4)
                act.activation(yst[0:rows_of(t), t % 2, :].rearrange("p (a b) -> p a b", a=2), ps[0:rows_of(t), b0:b0 + 2, :], ACT.Copy).then_inc(y_done, 1)

        @block.gpsimd
        def _(pool):
            def lo(l, ph, i, c, n=1024):
                hold(pool, "pool", units_hi, unit0(l, ph) + 6 * i + c + 1)
                pool.tensor_tensor(w_lo[:, c % 6, 0:n], raw[:, c % 3, 0:n], w_hi[:, c % 6, 0:n].bitcast(F32), ALU.subtract).then_inc(units_split, 1)

            def ffn(l, ph):
                for c in range(4):
                    lo(l, ph, 0, c)
                with pool.Fori(0, FB - 1) as j:
                    for c in range(4, 10):
                        lo(l, ph, j, c)
                for c in range(U_FFN - 2, U_FFN):
                    lo(l, ph, 0, c)

            pool.memset(pw[:, :, :], 0.0).then_inc(zeroed, 1)
            pool.wait_ge(tiles, T_START)
            pool.sem_inc(units_split, RAW_SLOTS)

            with pool.Fori(0, DEPTH) as l:
                ffn(l, 0)
                steps = [0]

                def link(ins):
                    steps[0] += 1
                    ins.then_inc(pool_chain, 1)
                    hold(pool, "pool", pool_chain, l * POOL_CHAIN + steps[0])

                new = lambda t, w: t.rearrange("p (b s) -> p b s", s=w)
                ucx_new, ext_new = new(ucx[:, 2 + SEQ:NUX], 6), new(pb[0][:, 15 + SEQ:NPX], 19)

                def conv_products(j):
                    hold(pool, "pool", z_done, l * 26 + (10, 26)[j])
                    hold(pool, "pool", st_done, l + 1)
                    if j == 1:
                        hold(pool, "pool", tiles, T(l, 'TL0'))
                    link(pool.memset(ucx[:, 0:2], 0.0))
                    link(pool.tensor_copy(ucx_new[:, :, 0:2], new(states[:, j, 120:136], 2)))
                    link(pool.tensor_tensor(ucx[:, 2:2 + SEQ], cz[:, 0, 0:SEQ], cz[:, 1, 0:SEQ], ALU.mult))
                    pool.tensor_tensor(ucx_new[:, :, 2:6], new(cz[:, 0, SEQ:TOK], DT), new(cz[:, 1, SEQ:TOK], DT), ALU.mult).then_inc(ucx_done, 1)
                    hold(pool, "pool", ucx_done, l * 2 + j + 1)

                def conv_sum(j):
                    hold(pool, "pool", s_scr, 16)
                    n = NUX - 2
                    t0, t1 = (t[:, 0:n] for t in conv_t)
                    tap = lambda q: lv[:, CONV_TAPS + 2 * q + j:CONV_TAPS + 2 * q + j + 1]
                    link(pool.tensor_scalar(t0, ucx[:, 0:n], tap(0), None, ALU.mult))
                    link(pool.tensor_scalar(t1, ucx[:, 1:n + 1], tap(1), None, ALU.mult))
                    link(pool.tensor_tensor(t0, t0, t1, ALU.add))
                    link(pool.tensor_scalar(t1, ucx[:, 2:n + 2], tap(2), None, ALU.mult))
                    link(pool.tensor_tensor(t0, t0, t1, ALU.add))
                    link(pool.tensor_tensor(cat[:, j, 0:SEQ], t0[:, 0:SEQ], cz[:, 2, 0:SEQ], ALU.mult))
                    link(pool.tensor_tensor(new(cat[:, j, SEQ:TOK], DT), new(conv_t[0][:, SEQ + 2:NUX], 6)[:, :, 0:DT],
                                            new(cz[:, 2, SEQ:TOK], DT), ALU.mult))

                def windows(j):
                    u, (e, s, w) = cz[:, 3, :], pb
                    link(pool.memset(e[:, 0:15], 0.0))
                    link(pool.tensor_copy(ext_new[:, :, 0:15], new(states[:, j, 0:120], 15)))
                    link(pool.tensor_copy(e[:, 15:15 + SEQ], u[:, 0:SEQ]))
                    link(pool.tensor_copy(ext_new[:, :, 15:19], new(u[:, SEQ:TOK], DT)))
                    link(pool.tensor_tensor(s[:, 1:NPX], e[:, 1:NPX], e[:, 0:NPX - 1], ALU.add))
                    if j == 0:
                        link(pool.tensor_tensor(w[64:P, 3:NPX], s[64:P, 3:NPX], s[64:P, 1:NPX - 2], ALU.add))
                    else:
                        link(pool.tensor_tensor(w[:, 3:NPX], s[:, 3:NPX], s[:, 1:NPX - 2], ALU.add))
                        link(pool.tensor_tensor(s[:, 7:NPX], w[:, 7:NPX], w[:, 3:NPX - 4], ALU.add))
                        link(pool.tensor_tensor(w[64:P, 15:NPX], s[64:P, 15:NPX], s[64:P, 7:NPX - 8], ALU.add))
                    link(pool.tensor_copy(w[0:64, 15:NPX], s[0:64, 15:NPX]))

                def pool_diff(j):
                    u, (d, m, w) = cz[:, 3, :], pb
                    link(pool.tensor_scalar(m[:, 15:NPX], w[:, 15:NPX], cst[:, CO['rwin'] + j:CO['rwin'] + j + 1], None, ALU.mult))
                    link(pool.tensor_tensor(m[:, 15:31], w[:, 15:31], cst[:, CO['rcnt'] + 16 * j:CO['rcnt'] + 16 * j + 16], ALU.mult))
                    link(pool.tensor_tensor(d[:, 0:SEQ], m[:, 15:15 + SEQ], u[:, 0:SEQ], ALU.subtract))
                    pool.tensor_tensor(new(d[:, SEQ:TOK], DT), new(m[:, 15 + SEQ:NPX], 19)[:, :, 15:19], new(u[:, SEQ:TOK], DT), ALU.subtract).then_inc(d_done, 1)
                    hold(pool, "pool", d_done, l * 2 + j + 1)

                for c in range(17):
                    lo(l, 1, 0, c, 512 if c < 4 else 1024)
                conv_products(0)
                lo(l, 1, 0, 17)
                conv_sum(0)
                lo(l, 1, 0, 18)
                windows(0)
                lo(l, 1, 0, 19)
                pool_diff(0)
                lo(l, 1, 0, 20)
                lo(l, 1, 0, 21)
                hold(pool, "pool", z_done, l * 26 + 14)
                hold(pool, "pool", tiles, T(l, 'SC'))
                link(pool.memset(qz[:, :, :, :], 0.0))
                for h in range(NH):
                    r = 64 * (h % 2)
                    ins = pool.tensor_copy(qz[r:r + 64, h // 2, :, DT * h:DT * (h + 1)], new(qT[r:r + 64, h // 2, SEQ:TOK], DT))
                    ins.then_inc(qz_done, 1)
                hold(pool, "pool", qz_done, (l + 1) * NH)
                for c in range(22, 28):
                    lo(l, 1, 0, c)
                hold(pool, "pool", tiles, T(l, 'U1'))
                pool.memset(keysT[:, :, PAST + DT:LS], 0.0).then_inc(keys_padded, 1)
                hold(pool, "pool", keys_padded, l + 1)
                conv_products(1)
                hold(pool, "pool", tiles, T(l, 'PM0'))
                conv_sum(1)
                windows(1)
                pool_diff(1)
                for g in range(2):
                    hold(pool, "pool", lg_done, l * 2 + g + 1)
                    pool.tensor_tensor(lg[:, g, :], lg[:, g, :], bias_s[:, :], ALU.add).then_inc(lgb_done, 1)
                for c in range(28, 36):
                    lo(l, 1, 0, c)
                assert steps[0] == POOL_CHAIN, steps
                ffn(l, 2)

        @block.vector
        def _(dve):
            def norm(l, k):
                dve.wait_ge(rt_done, k + 1)
                dve.reciprocal(rstd[:, :], rstd[:, :]).then_inc(rstd_done, 1)
                dve.wait_ge(rstd_done, k + 1)
                for c in range(KC):
                    if c >= 2:
                        dve.wait_ge(h_ready if l is not None else hhi_done, k * KC + c - 1)
                    dve.tensor_tensor(normed[:, c % 2, :], xT[:, c, :], rstd[:, :], ALU.mult).then_inc(normed_done, 1)
                    if c >= 1 and l is not None:
                        low(l[0], l[1], k, c - 1)
                if l is not None:
                    low(l[0], l[1], k, KC - 1)

            def low(l, ph, k, c):
                dve.wait_ge(hhi_done, k * KC + c + 1)
                dve.scalar_tensor_tensor(h_lo[:, c, :], normed[:, c % 2, :], lv[:, 8 * ph + c:8 * ph + c + 1],
                                         h_hi[:, c, :].bitcast(F32), ALU.mult, ALU.subtract).then_inc(h_ready, 1)

            def ffn(l, f):
                ph = 2 * f
                t0, s0, xb = tile0(l, ph), (l * 2 + f) * 2 * FB, x0(l, ph)
                norm((l, ph), norm_no(l, ph))

                def gate_up(i, tile, again):
                    for m in range(2):
                        dve.wait_ge(silu_done, s0 + 2 * i + m + 1)
                        if again:
                            dve.wait_ge(act_ready, s0 + 2 * i + m - 1)
                        dve.wait_ge(tiles, tile + m)
                        dve.tensor_tensor(halves(gated[:, m, :]), pair(2 + m), halves(silu[:, m, :]), ALU.mult).then_inc(gu_done, 1)

                def act_low(i):
                    for m in range(2):
                        dve.wait_ge(acthi_done, s0 + 2 * i + m + 1)
                        dve.tensor_tensor(act_lo[:, m, :], gated[:, m, :], act_hi[:, m, :].bitcast(F32), ALU.subtract).then_inc(act_ready, 1)

                def add_down(i, tile):
                    for c in range(KC):
                        dve.wait_ge(x_updates, xb + 8 * i)
                        dve.wait_ge(tiles, tile + c)
                        dve.scalar_tensor_tensor(halves(xT[:, c, :]), pair(c % 4), 0.5, halves(xT[:, c, :]), ALU.mult, ALU.add).then_inc(x_updates, 1)

                gate_up(0, t0 + 4, False)
                act_low(0)
                with dve.Fori(0, FB - 1) as j:
                    gate_up(j + 1, t0 + 12 * j + 8, True)
                    add_down(j, t0 + 12 * j + 10)
                    act_low(j + 1)
                add_down(FB - 1, t0 + T_FFN - 7)

            dve.memset(epsb[:, :], EPS).then_inc(zeroed, 1)
            dve.memset(relx[:, :, :], 0.0).then_inc(relx_done, 1)
            dve.wait_ge(s_in, 16 * S_IN)
            dve.wait_ge(relx_done, 1)
            for t in range(DT):
                for b in range(4):
                    dve.tensor_copy(relx[:, t, :].rearrange("p (b h t) -> p b h t", b=4, h=NH)[:, b, :, t], rel_sb[:, :]).then_inc(relx_done, 1)
            for t in range(5):
                dve.wait_ge(tiles, t + 1)
                r = rows_of(t)
                dve.tensor_copy(xT[:, :, t * P:t * P + r].rearrange("p (a c) n -> p a c n", a=2),
                                ps[:, 2 * (t % 4):2 * (t % 4) + 2, :].rearrange("p a (c n) -> p a c n", n=P)[:, :, :, 0:r]).then_inc(x_updates, 1)
            dve.wait_ge(tiles, 6)
            dve.tensor_copy(vecs[:, :], ps[:, 2, 0:DEPTH * 32 + 8]).then_inc(zeroed, 1)
            dve.wait_ge(tiles, 8)
            dve.tensor_copy(bias_s[:, :].rearrange("p (a b) -> p a b", a=3), ps[:, 0:3, 0:LT]).then_inc(zeroed, 1)
            dve.sem_inc(topk, 3)
            dve.wait_ge(zeroed, 4)

            with dve.Fori(0, DEPTH) as l:
                dve.tensor_copy(lv[:, :], vecs[:, ds(l * 32, 32)]).then_inc(lv_done, 1)
                hold(dve, "dve", lv_done, l + 1)
                ffn(l, 0)
                norm((l, 1), norm_no(l, 1))
                dve.wait_ge(tiles, T(l, 'WT'))
                dve.tensor_scalar(wi_nat[:, :, :], ps[:, 0, 0:4 * P].rearrange("p (t r) -> p t r", t=4)[:, :, P - IH:P], IH ** -0.5, None, ALU.mult).then_inc(wt_done, 1)
                for g in range(2):
                    dve.tensor_tensor(wsel[:, g, :], ps[:, 1, 0:32], C('own_query', n=32, off=32 * g), ALU.mult).then_inc(wt_done, 1)
                q4 = qis[:, :, :].rearrange("p b (c e t) -> p b c e t", e=2, t=DT)
                for e in range(2):
                    for c in range(4):
                        src = (qi[0:ID, c, SEQ:TOK] if e == 0 else ps[0:ID, 1, 32 * (c + 1):32 * (c + 2)])
                        last = dve.tensor_copy(q4[:, :, c, e, :], src.rearrange("p (b t) -> p b t", t=DT))
                        if c == 3:
                            last.then_inc(wt_done, 1)
                dve.memset(kidxT[:, :, PAST + DT:LS], 0.0).then_inc(wt_done, 1)
                dve.wait_ge(wt_done, l * 6 + 6)
                for n in range(12):
                    qb, c = 1 + n // 4, n % 4
                    L = (qb + 1) * P
                    work = work_p[:, WOFF[qb]:WOFF[qb] + L]
                    for e in range(2):
                        w = wi_nat[:, qb, 2 * c + e:2 * c + e + 1]
                        dve.wait_ge(relu_done, l * 12 + n + 1)
                        if c == e == 0:
                            dve.tensor_scalar(work, prelu[:, n % 2, e, 0:L], w, None, ALU.mult).then_inc(iacc_done, 1)
                        else:
                            dve.wait_ge(iacc_done, l * 27 + 2 * n + e)
                            dve.scalar_tensor_tensor(work, prelu[:, n % 2, e, 0:L], w, work, ALU.mult, ALU.add).then_inc(iacc_done, 1)
                dve.wait_ge(iacc_done, l * 27 + 24)
                for qb in range(1, QB):
                    diag = work_p[:, WOFF[qb] + qb * P:WOFF[qb] + (qb + 1) * P]
                    dve.tensor_tensor(diag, diag, C('causal'), ALU.add).then_inc(iacc_done, 1)
                hold(dve, "dve", iacc_done, l * 27 + 27)
                with dve.Fori(0, TOPK_P // 8) as r:
                    for n in range(6):
                        qb = 1 + n % 3
                        work = work_p[:, WOFF[qb]:WOFF[qb] + (qb + 1) * P]
                        hold(dve, "dve", topk, l * TOPK_STEPS + r * 6 + n + 1)
                        if n < 3:
                            dve.max(top8[:, n, :], work).then_inc(topk, 1)
                        else:
                            dve.match_replace(work, top8[:, n - 3, :], work, TAKEN).then_inc(topk, 1)
                hold(dve, "dve", sc_done, l + 1)
                dve.tensor_tensor(work_s[:, PAST:LS], work_s[:, PAST:LS], C('causal_new', 32), ALU.add).then_inc(masks_done, 1)
                hold(dve, "dve", masks_done, l * 3 + 1)
                with dve.Fori(0, TOPK_S // 8) as r:
                    hold(dve, "dve", topk, l * TOPK_STEPS + 96 + r * 2 + 3)
                    dve.max(top8[0:32, 0, :], work_s[:, :]).then_inc(topk, 1)
                    hold(dve, "dve", topk, l * TOPK_STEPS + 96 + r * 2 + 4)
                    dve.match_replace(work_s[:, :], top8[0:32, 0, :], work_s[:, :], TAKEN).then_inc(topk, 1)
                hold(dve, "dve", topk, (l + 1) * TOPK_STEPS + 3)
                for work in (work_s, work_p):
                    dve.tensor_scalar(work[:, :], work[:, :], TAKEN / 2, NEG, ALU.is_gt, ALU.mult).then_inc(masks_done, 1)

                def s_logits(g):
                    b0 = (4, 0)[g]
                    hold(dve, "dve", lgb_done, l * 2 + g + 1)
                    hold(dve, "dve", tiles, T(l, f'MX{g}'))
                    row = lg[:, g, :].rearrange("p (a b) -> p a b", a=3)
                    dve.tensor_tensor_reduce(out=row, in0=ps[:, b0:b0 + 3, 0:LT], in1=row, scale=1.0, scalar=2 * NEG, op0=ALU.add, op1=ALU.max,
                                             accum_out=sstat[:, g, 0:1]).then_inc(slog_done, 1)
                    dve.wait_ge(slog_done, l * 4 + 2 * g + 1)
                    dve.tensor_scalar(sstat[:, g, 1:2], sstat[:, g, 0:1], -1.0, None, ALU.mult).then_inc(slog_done, 1)

                def s_norm(g):
                    n0 = l * 6 + 3 * g
                    dve.wait_ge(sexp_done, l * 2 + g + 1)
                    dve.reciprocal(sstat[:, g, 3:4], sstat[:, g, 2:3]).then_inc(snorm_done, 1)
                    dve.wait_ge(snorm_done, n0 + 1)
                    dve.tensor_scalar(lg[:, g, :], lg[:, g, :], sstat[:, g, 3:4], None, ALU.mult).then_inc(snorm_done, 1)
                    dve.wait_ge(snorm_done, n0 + 2)
                    if g == 1:
                        dve.wait_ge(tiles, T(l, 'PTN0'))
                    new_p = lg[:, g, PAST:PAST + DT].unsqueeze(1).to_broadcast([P, DB, DT])
                    dve.tensor_tensor(pnew[:, :].rearrange("p (b t) -> p b t", t=DT), new_p,
                                      C('own_batch', n=32, off=32 * g).rearrange("p (b t) -> p b t", t=DT), ALU.mult).then_inc(snorm_done, 1)

                def s_transposed(g):
                    if g == 1:
                        dve.wait_ge(sout_mm, l * DB + 4)
                    dve.wait_ge(tiles, T(l, f'PTR{g}'))
                    dve.tensor_copy(pTs[:, :, :].rearrange("p (a k) n -> p a (k n)", a=2), pair((2, 0)[g], P, 512)).then_inc(ptr_done, 1)
                    dve.wait_ge(tiles, T(l, f'PTN{g}'))
                    dve.tensor_copy(pTn[:, :], ps[0:32, (6, 2)[g], 0:P]).then_inc(ptr_done, 1)

                def s_out(g):
                    dve.wait_ge(sout_mm, l * DB + 4 * g + 4)
                    for e in range(2):
                        r = slice(64 * e, 64 * e + 64)
                        src = ps[r, (7, 3)[g], 0:P].rearrange("p (c b q) -> p c b q", c=4, b=4)[:, :, :, DT * e:DT * e + DT]
                        dst = cat[r, 4:8, SEQ + 16 * g:SEQ + 16 * g + 16].rearrange("p c (b t) -> p c b t", t=DT)
                        dve.tensor_copy(dst, src).then_inc(sout_done, 1)

                s_logits(0)
                s_logits(1)
                s_norm(0)
                s_transposed(0)
                s_norm(1)
                s_out(0)
                s_transposed(1)
                s_out(1)

                def p_logits(n):
                    qb, c = n // 4, n % 4
                    L = (qb + 1) * P
                    if n == 0:
                        hold(dve, "dve", strip_loaded, (l + 1) * 16 * NH)
                        hold(dve, "dve", out_nat[0], (l + 1) * 96)
                        hold(dve, "dve", out_nat[1], (l + 1) * 64)
                        hold(dve, "dve", out_small, (l + 1) * 16 * OUT_SMALL + 16)
                    if n >= 2:
                        dve.wait_ge(tiles, T(l, f'PT{n - 2}'))
                    dve.wait_ge(tiles, T(l, f'PL{n}'))
                    dve.scalar_tensor_tensor(probs[:, n % 2, :, 0:L], pair(n % 2, P, L), SCALE,
                                             strip[:, 2 * c:2 * c + 2, SEQ - L:SEQ], ALU.mult, ALU.add).then_inc(plog_done, 1)
                    hold(dve, "dve", plog_done, l * 64 + 4 * n + 1)
                    mask = C('causal') if qb == 0 else work_p[:, WOFF[qb]:WOFF[qb] + L]
                    for e in range(2):
                        row = probs[:, n % 2, e, 0:L]
                        dve.tensor_tensor_reduce(out=row, in0=row, in1=mask, scale=1.0, scalar=2 * NEG, op0=ALU.add, op1=ALU.max,
                                                 accum_out=stat[:, n % 2, e:e + 1]).then_inc(plog_done, 1)
                    dve.wait_ge(plog_done, l * 64 + 4 * n + 3)
                    dve.tensor_scalar(stat[:, n % 2, 2:4], stat[:, n % 2, 0:2], -1.0, None, ALU.mult).then_inc(plog_done, 1)

                def p_norm(n):
                    L = (n // 4 + 1) * P
                    dve.wait_ge(pexp_done, l * 32 + 2 * n + 2)
                    dve.reciprocal(stat[:, n % 2, 6:8], stat[:, n % 2, 4:6]).then_inc(pnorm_done, 1)
                    dve.wait_ge(pnorm_done, l * 48 + 3 * n + 1)
                    for e in range(2):
                        row = probs[:, n % 2, e, 0:L]
                        dve.tensor_scalar(row, row, stat[:, n % 2, 6 + e:7 + e], None, ALU.mult).then_inc(pnorm_done, 1)

                for n in range(17):
                    if n < 16:
                        p_logits(n)
                    if n >= 1:
                        p_norm(n - 1)
                for c in range(KC):
                    dve.wait_ge(cathi_done, l * KC + c + 1)
                    dve.tensor_tensor(h_lo[:, c, :], cat[:, c, :], h_hi[:, c, :].bitcast(F32), ALU.subtract).then_inc(cat_ready, 1)
                for c in range(KC):
                    dve.wait_ge(tiles, T(l, f'WO{c}'))
                    dve.tensor_tensor(halves(xT[:, c, :]), pair(c % 4), halves(xT[:, c, :]), ALU.add).then_inc(x_updates, 1)
                ffn(l, 1)
            norm(None, 3 * DEPTH)

        @block.tensor
        def _(pe):
            ones = C('ones')

            def split_ready(l, ph, i, c):
                pe.wait_ge(units_split, unit0(l, ph) + 6 * i + c + 1 + RAW_SLOTS)

            def product(out, w0, w1, xh, xl, first, last):
                for w, x in ((w0, xh), (w0, xl), (w1, xh)):
                    for hf in range(2):
                        ins = pe.matmul(out[:, hf, :], w, x[:, HT * hf:HT * (hf + 1)],
                                        start=first and w is w0 and x is xh, stop=last and w is w1)
                return ins

            def unit_tile(c, p, ks, wait_h=None, first=True, last=True):
                wh, wl = (w[:, c % 6, 0:P * len(ks)].rearrange("p (k n) -> p k n", k=len(ks)) for w in (w_hi, w_lo))
                for n, k in enumerate(ks):
                    if wait_h is not None:
                        pe.wait_ge(h_ready, wait_h + k + 1)
                    ins = product(pair(p), wh[:, n, :], wl[:, n, :], h_hi[:, k, :], h_lo[:, k, :],
                                  first and n == 0, last and n == len(ks) - 1)
                return ins

            def stats(k, xready):
                pe.wait_ge(x_updates, xready - 3)
                for c in range(KC):
                    pe.wait_ge(sq_done, k * KC + c + 1)
                    for hf in range(2):
                        ins = pe.matmul(pair(0)[:, hf, :], ones, sq[:, c, HT * hf:HT * (hf + 1)], start=c == 0, stop=c == KC - 1)
                ins.then_inc(tiles, 1)

            def ffn(l, f):
                ph = 2 * f
                s0, xb, nh = (l * 2 + f) * 2 * FB, x0(l, ph), norm_no(l, ph) * KC
                stats(norm_no(l, ph), xb)

                def gate_up(i, j, c0, again):
                    for p in range(4):
                        split_ready(l, ph, j, c0 + p)
                        if again:
                            pe.wait_ge(silu_done if p < 2 else gu_done, s0 + 2 * i + p % 2 - 1)
                            pe.wait_ge(x_updates, xb + 8 * i - 8)
                        ins = unit_tile(c0 + p, p, range(KC), wait_h=nh if not again and p == 0 else None)
                        ins.then_inc(tiles, 1)

                def down(i, j, c0, final):
                    split_ready(l, ph, j, c0 + 1)
                    pe.wait_ge(act_ready, s0 + 2 * i + 2)
                    for c in range(KC):
                        p = c % 4
                        if c >= 4 or final:
                            pe.wait_ge(x_updates, xb + 8 * i + c - 3)
                        else:
                            pe.wait_ge(silu_done if p < 2 else gu_done, s0 + 2 * i + 3 + p % 2)
                        for m in range(2):
                            wh, wl = (w[:, (c0 + m) % 6, c * P:(c + 1) * P] for w in (w_hi, w_lo))
                            ins = product(pair(p), wh, wl, act_hi[:, m, :], act_lo[:, m, :], m == 0, m == 1)
                        ins.then_inc(tiles, 1)

                gate_up(0, 0, 0, False)
                with pe.Fori(0, FB - 1) as j:
                    gate_up(j + 1, j, 4, True)
                    down(j, j, 8, False)
                down(FB - 1, 0, U_FFN - 2, True)

            pe.wait_ge(s_in, 16 * S_IN)
            for t in range(5):
                r = rows_of(t)
                pe.wait_ge(s_xrow[t % 2], 16 * (t // 2 + 1))
                if t == 4:
                    pe.wait_ge(x_updates, 1)
                for c in range(KC):
                    ins = pe.transpose(ps[:, 2 * (t % 4) + c // 4, P * (c % 4):P * (c % 4) + r], yst[0:r, t % 2, c * P:(c + 1) * P], ident[0:r, 0:r])
                ins.then_inc(tiles, 1)
            nv = DEPTH * 32 + 8
            pe.wait_ge(x_updates, 2)
            pe.transpose(ps[:, 2, 0:nv], vrows[0:nv, :], ident[0:nv, 0:nv]).then_inc(tiles, 1)
            pe.wait_ge(s_oh, 16)
            pe.wait_ge(x_updates, 3)
            pe.matmul(ps[0:NH, 4, :], rel_sb[:, :], oh[:, NTD:NTD + 512], start=True, stop=True)
            pe.matmul(ps[0:NH, 5, 0:NTP - 512], rel_sb[:, :], oh[:, NTD + 512:NTD + NTP], start=True, stop=True).then_inc(tiles, 1)
            pe.wait_ge(x_updates, 5)
            pe.wait_ge(zeroed, 3)
            pe.wait_ge(relx_done, 1 + 4 * DT)
            for b in range(3):
                for t in range(DT):
                    ins = pe.matmul(ps[:, b, 0:LT], relx[:, t, :], oh[:, DT - 1 - t + LT * b:DT - 1 - t + LT * (b + 1)], start=t == 0, stop=t == DT - 1)
            ins.then_inc(tiles, 1)

            with pe.Fori(0, DEPTH) as l:
                ffn(l, 0)
                stats(norm_no(l, 1), x0(l, 1))
                hold(pe, "pe", st_loaded, (l + 1) * 32)
                for j in range(2):
                    pe.transpose(ps[:, 2 + j, 0:120], srow[0:120, 0, j * P:(j + 1) * P], ident[0:120, 0:120])
                    ins = pe.transpose(ps[:, 2 + j, 120:136], srow[0:16, 1, j * P:(j + 1) * P], ident[0:16, 0:16])
                ins.then_inc(tiles, 1)

                for n in range(2):
                    for q in range(2):
                        split_ready(l, 1, 0, 2 * n + q)
                        ins = unit_tile(2 * n + q, 2 + n, range(4 * q, 4 * q + 4), wait_h=norm_no(l, 1) * KC if n == 0 else None,
                                        first=q == 0, last=q == 1)
                    ins.then_inc(tiles, 1)

                def z(n):
                    split_ready(l, 1, 0, n + 2)
                    unit_tile(n + 2, (n + 2) % 4, range(KC)).then_inc(tiles, 1)

                for n in range(2, 6):
                    if n == 3:
                        pe.wait_ge(st_done, l + 1)
                    if n >= 4:
                        pe.wait_ge(z_done, l * 26 + n - 3)
                    z(n)
                hold(pe, "pe", z_done, l * 26 + 6)
                for t in range(4):
                    pe.transpose(ps[:, 0, P * t:P * (t + 1)], wi[:, P * t:P * (t + 1)], ident)
                pe.matmul(ps[:, 1, 0:NEWROWS], C('head_of'), wi[:, SEQ:TOK], start=True, stop=True)
                for c in range(4):
                    ins = pe.matmul(ps[0:ID, 1, 32 * (c + 1):32 * (c + 2)], ident[64:P, 64:P], qi[64:P, c, SEQ:TOK], start=True, stop=True)
                ins.then_inc(tiles, 1)

                for n in range(12):
                    qb, c, L = 1 + n // 4, n % 4, (2 + n // 4) * P
                    if n >= 2:
                        hold(pe, "pe", relu_done, l * 12 + n - 1)
                    for e in range(2):
                        r = slice(64 * e, 64 * e + 64)
                        ins = pe.matmul(ps[:, 4 + 2 * (n % 2) + e, 0:L], qi[r, c, qb * P:(qb + 1) * P], ki[r, 0:L], start=True, stop=True)
                    ins.then_inc(tiles, 1)

                def index_keys(b):
                    hold(pe, "pe", kidx_loaded[b % 2], l * 4 * 16 * NPG + (b // 2 + 1) * 16 * NPG)
                    hold(pe, "pe", relu_done if b < 2 else kit_done, (l * 12 + 11 + b) if b < 2 else (l * 16 + 2 * b - 3))
                    for pg in range(NPG):
                        ins = pe.transpose(ps[0:ID, 4 + 2 * (b % 2) + pg // 4, P * (pg % 4):P * (pg % 4) + P], kipages[:, b % 2, pg, :], ident)
                    ins.then_inc(tiles, 1)

                index_keys(0)
                for b in range(DB):
                    if b < DB - 1:
                        index_keys(b + 1)
                    if b == 0:
                        hold(pe, "pe", wt_done, l * 6 + 6)
                    if b == 4:
                        hold(pe, "pe", srelu_done, l * 2 + 1)
                    hold(pe, "pe", kit_done, l * 16 + 2 * b + 2)
                    r = 32 * (b % 4)
                    for t in range(3):
                        ins = pe.matmul(ps[r:r + 32, t, 0:LT], qis[:, b, :], kidxT[:, b % 2, LT * t:LT * (t + 1)], start=True, stop=True)
                    ins.then_inc(score_mm, 1)
                hold(pe, "pe", srelu_done, l * 2 + 2)
                for t in range(3):
                    for g in range(2):
                        ins = pe.matmul(ps[0:32, 4 + t, 0:LT], wsel[:, g, :], srelu[:, g, t, :], start=g == 0, stop=g == 1)
                ins.then_inc(tiles, 1)

                def tail(j):
                    hold(pe, "pe", ucx_done, l * 2 + j + 1)
                    pe.transpose(ps[0:47, 0, 0:P], cz[:, 3, TAIL:TOK], ident)
                    pe.transpose(ps[0:6 * DB, 1, 0:P], ucx[:, 2 + SEQ:NUX], ident)
                    pe.transpose(ps[0:2, 1, P:2 * P], ucx[:, SEQ:SEQ + 2], ident).then_inc(tiles, 1)

                def pool_product(j):
                    hold(pe, "pe", pw_loaded, (l + 1) * 64)
                    hold(pe, "pe", d_done, l * 2 + j + 1)
                    for hf in range(2):
                        ins = pe.matmul(pair(1)[:, hf, :], pw[:, j, :], pb[0][:, HT * hf:HT * (hf + 1)], start=True, stop=True)
                    ins.then_inc(tiles, 1)

                for n in range(6, 18):
                    if n in (8, 9):
                        pe.wait_ge(sc_done, l + 1)
                    if n >= 10:
                        pe.wait_ge(z_done, l * 26 + n - 3)
                    z(n)
                hold(pe, "pe", z_done, l * 26 + 16)
                tail(0)
                pool_product(0)
                for n in range(18, 22):
                    if n == 18:
                        pe.wait_ge(tail_done, l * 6 + 3)
                    elif n == 19:
                        pe.wait_ge(pm_done, l * 2 + 1)
                    else:
                        pe.wait_ge(z_done, l * 26 + n - 3)
                    z(n)
                hold(pe, "pe", z_done, l * 26 + 22)
                for t in range(5):
                    r = rows_of(t)
                    ins = pe.transpose(ps[0:r, 0, ID * t:ID * (t + 1)], ki[0:ID, P * t:P * t + r], ident[0:ID, 0:ID])
                ins.then_inc(tiles, 1)
                for t in range(5):
                    r, bank = rows_of(t), 2 * ((t + 1) % 4)
                    if t == 3:
                        hold(pe, "pe", kin_done, l * 2 + 2)
                    if t == 4:
                        hold(pe, "pe", nat_done, l * 10 + 2)
                    for q, src in enumerate((kT, cz)):
                        for c in range(4):
                            ins = pe.transpose(ps[0:r, bank + q, P * c:P * (c + 1)], src[:, c, P * t:P * t + r], ident)
                    ins.then_inc(tiles, 1)
                for n in range(22, 26):
                    if n < 24:
                        pe.wait_ge(nat_done, l * 10 + 2 * (n - 18))
                    z(n)

                def key_tile(b, j):
                    m = 4 * b + j
                    if m < 2:
                        hold(pe, "pe", z_done, l * 26 + 25 + m)
                    else:
                        hold(pe, "pe", keys_done, l * 40 + 5 * ((m - 2) // 4) + (m - 2) % 4 + 1)
                    if j % 2 == 0:
                        hold(pe, "pe", k_loaded[j // 2], l * DB * 64 + (b + 1) * 64)
                    for pg in (2 * j, 2 * j + 1):
                        for c in range(4):
                            col = 256 * (c % 2) + P * (pg % 2)
                            ins = pe.transpose(ps[:, 4 + 2 * (j % 2) + c // 2, col:col + P], kpages[:, pg, P * c:P * (c + 1)], ident)
                    ins.then_inc(tiles, 1)

                def logits(b):
                    if b == 0:
                        hold(pe, "pe", qz_done, (l + 1) * NH)
                        hold(pe, "pe", keys_padded, l + 1)
                    if b == 4:
                        hold(pe, "pe", pm_done, l * 2 + 2)
                    hold(pe, "pe", keys_done, l * 40 + 5 * b + 5)
                    r = 32 * (b % 4)
                    for t in range(3):
                        for c in range(4):
                            ins = pe.matmul(ps[r:r + 32, t, 0:LT], qz[:, c, b, :], keysT[:, c, LT * t:LT * (t + 1)], start=c == 0, stop=c == 3)
                    ins.then_inc(logit_mm, 1)

                for j in range(4):
                    key_tile(0, j)
                for b in range(DB):
                    if b < DB - 1:
                        key_tile(b + 1, 0)
                        key_tile(b + 1, 1)
                    logits(b)
                    if b == 3:
                        hold(pe, "pe", lg_done, l * 2 + 1)
                        tail(1)
                        pool_product(1)
                    if b < DB - 1:
                        key_tile(b + 1, 2)
                        key_tile(b + 1, 3)
                hold(pe, "pe", masks_done, l * 3 + 2)
                hold(pe, "pe", keys_done, l * 40 + 40)
                hold(pe, "pe", lg_done, l * 2 + 2)
                for g in range(2):
                    for t in range(3):
                        ins = pe.matmul(ps[:, (4, 0)[g] + t, 0:LT], C('row_of', 32, P, P * g), work_s[:, LT * t:LT * (t + 1)], start=True, stop=True)
                    ins.then_inc(tiles, 1)

                for g in range(2):
                    hold(pe, "pe", snorm_done, l * 6 + 3 * g + 3)
                    for pg in range(NPG):
                        ins = pe.transpose(ps[:, (4, 0)[g] + pg // 4, P * (pg % 4):P * (pg % 4) + P], lg[:, g, P * pg:P * (pg + 1)], ident)
                    ins.then_inc(tiles, 1)
                    pe.transpose(ps[0:32, (6, 2)[g], 0:P], pnew[:, :], ident).then_inc(tiles, 1)
                    hold(pe, "pe", ptr_done, l * 4 + 2 * g + 2)
                    for q in range(4):
                        b = 4 * g + q
                        hold(pe, "pe", v_loaded[b % 2], l * 4 * 16 * NPG + (b // 2 + 1) * 16 * NPG)
                        for c in range(4):
                            out = ps[:, (7, 3)[g], 8 * (4 * c + q):8 * (4 * c + q) + 8]
                            mine = slice(32 * q + 8 * c, 32 * q + 8 * c + 8)
                            for pg in range(NPG):
                                pe.matmul(out, vpages[b % 2][:, pg, P * c:P * (c + 1)], pTs[:, pg, mine], start=pg == 0, stop=False)
                            ins = pe.matmul(out, vn[0:NEWROWS, 4, P * c:P * (c + 1)], pTn[:, mine], start=False, stop=True)
                        ins.then_inc(sout_mm, 1)

                hold(pe, "pe", sout_done, l * 4 + 4)
                for n in range(18):
                    if n < 16:
                        qb, c, L = n // 4, n % 4, (n // 4 + 1) * P
                        if n >= 2:
                            hold(pe, "pe", plog_done, l * 64 + 4 * (n - 2) + 1)
                        for e in range(2):
                            r = slice(64 * e, 64 * e + 64)
                            ins = pe.matmul(pair(n % 2, P, L)[:, e, :], qT[r, c, qb * P:(qb + 1) * P], kT[r, c, 0:L], start=True, stop=True)
                        ins.then_inc(tiles, 1)
                    if 1 <= n < 17:
                        m = n - 1
                        hold(pe, "pe", pnorm_done, l * 48 + 3 * m + 3)
                        if m >= 1:
                            hold(pe, "pe", ppt_done, l * 16 + m)
                        for e in range(2):
                            for kb in range(m // 4 + 1):
                                ins = pe.transpose(ps[:, 4 + e, P * kb:P * (kb + 1)], probs[:, m % 2, e, P * kb:P * (kb + 1)], ident)
                        ins.then_inc(tiles, 1)
                    if n >= 2:
                        m = n - 2
                        hold(pe, "pe", ppt_done, l * 16 + m + 1)
                        if m >= 1:
                            hold(pe, "pe", po_done, l * 16 + m)
                        for e in range(2):
                            h = 2 * (m % 4) + e
                            for kb in range(m // 4 + 1):
                                ins = pe.matmul(ps[64 * e:64 * e + 64, 6, 0:P], vn[:, kb, HD * h:HD * (h + 1)], pTp[:, e, P * kb:P * (kb + 1)],
                                                start=kb == 0, stop=kb == m // 4)
                        ins.then_inc(tiles, 1)

                for n in range(8):
                    split_ready(l, 1, 0, 28 + n)
                    if n == 0:
                        pe.wait_ge(cat_ready, (l + 1) * KC)
                    if n >= 4:
                        pe.wait_ge(x_updates, x0(l, 1) + n - 3)
                    unit_tile(28 + n, n % 4, range(KC)).then_inc(tiles, 1)
                ffn(l, 1)

            stats(3 * DEPTH, X_START + DEPTH * X_LAYER)
            pe.wait_ge(hhi_done, (3 * DEPTH + 1) * KC)
            for t in range(5):
                r = rows_of(t)
                if t == 4:
                    pe.wait_ge(y_done, 1)
                for c in range(KC):
                    ins = pe.transpose(ps[0:r, 2 * (t % 4) + c // 4, P * (c % 4):P * (c % 4) + P], sq[:, c, t * P:t * P + r], ident)
                ins.then_inc(tiles, 1)


_INS = ['x_prompt', 'x_sample', 'cache_k', 'cache_v', 'cache_kidx', 'state_conv', 'state_pool', 'page_table',
        'norm_ffn1', 'ffn1_gate', 'ffn1_up', 'ffn1_down', 'norm_mix', 'w_in', 'conv_w', 'pool_w', 'pool_scale', 'w_o',
        'norm_ffn2', 'ffn2_gate', 'ffn2_up', 'ffn2_down', 'rel_bias', 'norm_final']
_OUTS = [('y_prompt', (1, SEQ, D)), ('y_sample', (DB, DT, D)),
         ('k_prompt', (DEPTH, 1, SEQ, NH, HD)), ('v_prompt', (DEPTH, 1, SEQ, NH, HD)), ('kidx_prompt', (DEPTH, 1, SEQ, ID)),
         ('conv_prompt', (DEPTH, 1, 2, WC)), ('pool_prompt', (DEPTH, 1, 15, WP)),
         ('k_sample', (DEPTH, DB, DT, NH, HD)), ('v_sample', (DEPTH, DB, DT, NH, HD)), ('kidx_sample', (DEPTH, DB, DT, ID)),
         ('conv_sample', (DEPTH, DB, 2, WC)), ('pool_sample', (DEPTH, DB, 15, WP))]


def kernel(**inputs):
    import concourse.bacc as _bacc
    from concourse.bass_utils import run_bass_kernel_spmd as _run

    nc = _bacc.Bacc("TRN2", target_bir_lowering=False, num_devices=1)
    arrays, aps = {}, {}
    given = {n: np.ascontiguousarray(inputs[n]) for n in _INS}
    given['consts'] = shape_constants()
    given['onehots'] = bucket_one_hots()
    for name, v in given.items():
        arrays[f"in_{name}"] = v
        aps[name] = nc.dram_tensor(f"in_{name}", v.shape, mybir.dt.from_np(v.dtype), kind="ExternalInput").ap()
    for name, shape in _OUTS:
        aps[name] = nc.dram_tensor(f"out_{name}", shape, F32, kind="ExternalOutput").ap()
    aps['scratch'] = nc.dram_tensor("bias_by_distance", (NH, P, NTP), F32, kind="Internal").ap()
    trunk(nc, aps)
    r = _run(nc, [arrays], core_ids=[0])
    return tuple(r.results[0][f"out_{name}"] for name, _ in _OUTS)
```

```python
from contextlib import ExitStack

import numpy as np
import concourse.bass as bass
from concourse import mybir

F32 = mybir.dt.float32
F32R = mybir.dt.float32r
I32 = mybir.dt.int32
ACT = mybir.ActivationFunctionType
ALU = mybir.AluOpType
ds = bass.ds

P = 128
D, SEQ, DEPTH, DB, DT, PAST, PAGE = 1024, 512, 2, 8, 4, 1024, 128
DFF, NH, HD, IH, ID = 2816, 8, 64, 8, 64
WC, WP, WA = 256, 256, 512
NPG = PAST // PAGE
TOK = SEQ + DB * DT
HT = TOK // 2
KC = D // P
FB = DFF // 256
EPS = 1e-6
TOPK_P, TOPK_S = 128, 256
LS = PAST + 8
LT = LS // 3
NEG = -1e30
TAKEN = -3e38
QB = SEQ // P
POOLW = (2, 4, 8, 16)
SCALE = HD ** -0.5
C_BG, C_CG, C_XIN, C_U, C_Q, C_K, C_V, C_QI, C_KI, D_IN = 0, 256, 512, 768, 1024, 1536, 2048, 2560, 3072, 3144
RAW_SLOTS, SPLIT_SLOTS = 3, 6

_CW = dict(ident=128, ones=128, causal=128, causal_new=8, row_of=256, head_of=128, own_query=64, own_batch=64,
           rwin=2, rcnt=32, own_head=8, out_of=16)
CO, _n = {}, 0
for _k, _w in _CW.items():
    CO[_k] = _n
    _n += _w
NCONST = _n
NTD, NTP = LS + DT - 1, SEQ + P - 1


def shape_constants():
    c = np.zeros((P, NCONST), np.float32)
    p = np.arange(P)
    c[:, CO['ident']:CO['ident'] + P] = np.eye(P)
    c[:, CO['ones']:CO['ones'] + P] = 1.0
    c[:, CO['causal']:CO['causal'] + P] = np.where(p[None, :] <= p[:, None], 0.0, NEG)
    j = np.arange(8)
    c[:DB * DT, CO['causal_new']:CO['causal_new'] + 8] = np.where(
        (j[None, :] <= np.arange(DB * DT)[:, None] % DT) & (j[None, :] < DT), 0.0, NEG)
    pb, ph, pt = p // 32, p % 32 // 4, p % 4
    bt = np.arange(32)
    for g in range(2):
        own_b = bt[:, None] // 4 == 4 * g + pb[None, :]
        own_bt = own_b & (bt[:, None] % 4 == pt[None, :])
        c[:32, CO['row_of'] + g * P:CO['row_of'] + (g + 1) * P] = own_bt
        c[:, CO['own_query'] + 32 * g:CO['own_query'] + 32 * g + 32] = own_bt.T * IH ** -0.5
        c[:, CO['own_batch'] + 32 * g:CO['own_batch'] + 32 * g + 32] = own_b.T
    c[:, CO['own_head']:CO['own_head'] + IH] = ph[:, None] == np.arange(IH)[None, :]
    c[:, CO['out_of']:CO['out_of'] + 16] = (pb * 4 + pt)[:, None] == np.arange(16)[None, :]
    c[P - IH:, CO['head_of']:CO['head_of'] + P] = np.arange(IH)[:, None] == ph[None, :]
    for jc in range(2):
        for half in range(2):
            w = POOLW[2 * jc + half]
            r = slice(64 * half, 64 * half + 64)
            c[r, CO['rwin'] + jc] = 1.0 / w
            c[r, CO['rcnt'] + 16 * jc:CO['rcnt'] + 16 * jc + 16] = 1.0 / np.minimum(w, np.arange(16) + 1)
    return c


def bucket_one_hots():
    dist = np.concatenate([PAST + DT - 1 - np.arange(NTD), SEQ - 1 - np.arange(NTP)])
    n = np.maximum(dist, 0)
    nf = np.maximum(n, 1).astype(np.float32)
    large = 16 + (np.log(nf / 16) / np.float32(np.log(8.0)) * 16).astype(np.int32)
    b = np.where(n < 16, n, np.minimum(large, 31))
    return (np.arange(32)[:, None] == b[None, :]).astype(np.float32)


Z_TILES = ['KI', 'WI', 'QI0', 'QI1', 'QI2', 'QI3',
           'CG0', 'XIN0', 'BG0', 'U0', 'Q0', 'Q1', 'Q2', 'Q3', 'K0', 'K1', 'K2', 'K3',
           'CG1', 'XIN1', 'BG1', 'U1', 'V0', 'V1', 'V2', 'V3']
Z_NO = {n: i for i, n in enumerate(Z_TILES)}
MIX = ['STATS', 'ST'] + Z_TILES[:6] + ['WT'] + [f'IS{n}' for n in range(12)]
MIX += [f'KIT{b}' for b in range(DB)] + ['SC'] + Z_TILES[6:18] + ['TL0', 'PM0'] + Z_TILES[18:]
MIX += ['KIN'] + [f'NT{n}' for n in range(5)]
for _b in range(DB):
    MIX += [f'KT{_b}_0', f'KT{_b}_1'] + ['TL1', 'PM1'] * (_b == 4) + [f'KT{_b}_2', f'KT{_b}_3']
MIX += ['MX0', 'MX1', 'PTR0', 'PTN0', 'PTR1', 'PTN1']
V_AT = {1: 0, 3: 1, 5: 2, 7: 3, 10: 4, 12: 5, 14: 6, 16: 7}
MIX += ['PL0']
for _n in range(18):
    MIX += [f'PL{_n + 1}'] * (_n < 15) + [f'PT{_n - 1}'] * (1 <= _n < 17) + [f'PO{_n - 2}'] * (_n >= 2) + ['SO0'] * (_n == 8)
MIX += ['SO1']
MIX += [f'WO{n}' for n in range(8)]
MIX_NO = {n: i for i, n in enumerate(MIX)}
assert len(MIX_NO) == len(MIX)

T_FFN = 1 + 4 + 12 * (FB - 1) + 8
T_MIX = len(MIX)
T_LAYER = 2 * T_FFN + T_MIX
T_START = 5 + 3
U_FFN, U_MIX = 6 * FB, 36
U_LAYER = 2 * U_FFN + U_MIX
X_LAYER = 8 * FB * 2 + 8
X_START = 5
TOPK_STEPS = 16 * 6 + 32 * 2
POOL_CHAIN = 43
OUT_SMALL = 10
S_IN = 3 + 5 * DEPTH


def trunk(nc, a):
    ctx = ExitStack()
    with ctx:
        sem_n = [0]

        def sem(name):
            sem_n[0] += 1
            return ctx.enter_context(nc.semaphore(name))

        base = 16512
        place = [base]

        def region(nbytes):
            at = place[0]
            place[0] += (nbytes + 31) // 32 * 32
            assert place[0] <= 229368, place[0]
            return at

        def at(name, shape, offset, dt=F32):
            return nc.alloc_sbuf_tensor_at(name, shape, dt, offset=offset)

        r_x, r_hhi, r_hlo = region(KC * TOK * 4), region(KC * TOK * 4), region(KC * TOK * 4)
        xT = at("xT", [P, KC, TOK], r_x)
        h_hi = at("h_hi", [P, KC, TOK], r_hhi, F32R)
        h_lo = at("h_lo", [P, KC, TOK], r_hlo, F32R)
        yT = at("yT", [P, KC, TOK], r_hlo)
        kpages0 = at("kpages0", [P, NPG, WA], r_hhi)
        keysT = at("keysT", [P, 4, LS], r_hlo)
        strip = at("strip", [P, NH, SEQ], r_hhi)
        r_cat = region(KC * TOK * 4)
        cat = at("cat", [P, KC, TOK], r_cat)
        act_hi = at("act_hi", [P, 2, TOK], r_cat, F32R)
        act_lo = at("act_lo", [P, 2, TOK], r_cat + 2 * TOK * 4, F32R)
        srelu = at("srelu", [P, 2, 3, LT], r_cat + 4 * TOK * 4)
        sq = at("sq", [P, 3, TOK], r_cat + 4 * TOK * 4)
        yst = at("yst", [P, 2, D], r_cat)
        r_sg = region(4 * TOK * 4)
        silu = at("silu", [P, 2, TOK], r_sg)
        gated = at("gated", [P, 2, TOK], r_sg + 2 * TOK * 4)
        normed = at("normed", [P, 4, TOK], r_sg)
        prelu = at("prelu", [P, 2, 2, SEQ], r_sg)
        v_sb = at("v_sb", [P, 4, TOK], r_sg)
        probs = at("probs", [P, 2, 2, SEQ], r_sg)
        r_raw = region(RAW_SLOTS * 4096)
        raw = at("raw", [P, RAW_SLOTS, 1024], r_raw)
        lg = at("lg", [P, 2, LS], r_raw)
        r_whi, r_wlo = region(SPLIT_SLOTS * 4096), region(SPLIT_SLOTS * 4096)
        w_hi = at("w_hi", [P, SPLIT_SLOTS, 1024], r_whi, F32R)
        w_lo = at("w_lo", [P, SPLIT_SLOTS, 1024], r_wlo, F32R)
        kpages = [kpages0, at("kpages1", [P, NPG, WA], r_wlo)]
        vpages = [at("vpages0", [P, NPG, WA], r_whi), at("vpages1", [P, NPG, WA], r_wlo), at("vpages2", [P, NPG, WA], r_hlo)]
        oh = at("oh", [32, NTD + NTP], r_whi)
        r_qk, r_q, r_cz = region(4 * TOK * 4), region(4 * TOK * 4), region(4 * TOK * 4)
        qi = at("qi", [P, 4, TOK], r_qk)
        kT = at("kT", [P, 4, TOK], r_qk)
        qT = at("qT", [P, 4, TOK], r_q)
        kipages = at("kipages", [P, DB, NPG, ID], r_q)
        cz = at("cz", [P, 4, TOK], r_cz)
        r_ws = region(LS * 4)
        pTs = [at("pTs0", [P, NPG, P], r_whi + 16384), at("pTs1", [P, NPG, P], r_cz)]
        pTn = [at("pTn0", [32, P], r_whi + 20480), at("pTn1", [32, P], r_ws + 2048)]
        kn_stage = at("kn_stage", [P, 4, WA], r_whi + 16384)
        kn_last = at("kn_last", [DB * DT, WA], r_wlo + 16384)
        o_own = at("o_own", [P, WA], r_ws)
        pnew = at("pnew", [P, 32], r_whi + 20992)
        pTp = at("pTp", [P, 2, SEQ], r_cz + 4096)
        ki = at("ki", [P, TOK], region(TOK * 4))
        wi = at("wi", [P, TOK], region(TOK * 4))
        NUX = 2 + SEQ + DB * 6
        ucx = at("ucx", [P, NUX], region(NUX * 4))
        NPX = 15 + SEQ + DB * 19
        r_pb = region(3 * 2720)
        pb = [at(f"pb{n}", [P, NPX], r_pb + 2720 * n) for n in range(3)]
        tp_sb = at("tp_sb", [NH, NTP], r_pb + 2720)
        conv_t = [at(f"conv_t{n}", [P, NUX], r_pb + 2720 * (1 + n)) for n in range(2)]
        qz = at("qz", [P, 4, DB, 32], r_cat + 4 * TOK * 4)
        work_p = at("work_p", [P, P * (2 + 3 + 4)], region(P * 9 * 4))
        work_s = at("work_s", [32, LS], r_ws)
        r_vn = region(5 * WA * 4)
        vn = at("vn", [P, 5, WA], r_vn)
        kidxT = at("kidxT", [ID, 2, LS], r_vn)
        bias_s = at("bias_s", [P, LS], region(LS * 4))
        cst = at("cst", [P, NCONST], region(NCONST * 4))
        rdiag = at("rdiag", [P, 5, P], r_pb)
        rtok = at("rtok", [P, 5], region(32))
        vecs = at("vecs", [P, DEPTH * 32 + 8], region((DEPTH * 32 + 8) * 4))
        lv = at("lv", [P, 32], region(128))
        states = at("states", [P, 2, 2 * 16 // 2 + 120], region(2 * 136 * 4))
        pw = at("pw", [P, 2, P], region(1024))
        wi_nat = at("wi_nat", [P, 4, IH], region(128))
        wsel = at("wsel", [P, 2, 32], region(256))
        qis = at("qis", [ID, DB, 32], region(1024))
        top8 = at("top8", [P, 3, 8], region(96))
        stat = at("stat", [P, 2, 8], region(64))
        sstat = at("sstat", [P, 2, 4], region(32))
        rel_sb = at("rel_sb", [32, NH], region(32))
        relx = at("relx", [32, DT, P], r_wlo + 4096)
        epsb = at("epsb", [P, 1], region(32))
        pt_sb = at("pt_sb", [1, DB * NPG], region(DB * NPG * 4), I32)
        vrows = at("vrows", [P, P], r_wlo + 8192)
        srow = at("srow", [P, 2, WC], r_vn + 4096)
        r_stage = r_cat + 4 * TOK * 4 + 4096
        tail_st = at("tail_st", [47, 2, P], r_stage + 1280)
        conv_st = at("conv_st", [6 * DB, 2, 2 * P], r_stage + 2304)
        ki_st = at("ki_st", [P, 5, ID], r_stage)

        C = lambda name, rows=P, n=None, off=0: cst[0:rows, CO[name] + off:CO[name] + off + (n or _CW[name])]
        ident = C('ident')
        halves = lambda ap: ap.rearrange("p (a b) -> p a b", a=2)
        WOFF = {1: 0, 2: 2 * P, 3: 5 * P}

        ps = ctx.enter_context(nc.psum_tensor("ps", [P, 8, 512], F32))
        pair = lambda p, rows=P, n=HT: ps[0:rows, 2 * p:2 * p + 2, 0:n]

        loaded = [sem(f"raw_loaded{r}") for r in range(RAW_SLOTS)]
        units_hi = sem("units_hi")
        units_split = sem("units_split")
        tiles = sem("tiles")
        x_updates = sem("x_updates")
        sq_done, ssum_done, rt_done, rms_done = sem("sq_done"), sem("ssum_done"), sem("rms_root_done"), sem("rms_done")
        rb_done = sem("rb_done")
        normed_done, hhi_done, h_ready = sem("normed_done"), sem("hhi_done"), sem("h_ready")
        gained = sem("gained")
        h_odd = sem("h_odd_ready")
        silu_done, gu_done = sem("silu_done"), sem("gu_done")
        acthi_done, act_ready = sem("acthi_done"), sem("act_ready")
        s_cst = sem("constants_loaded")
        s_in, s_oh, s_scr = sem("start_loads"), sem("onehots_loaded"), sem("bias_scratch")
        s_xrow = [sem("xrow0"), sem("xrow1")]
        zeroed, relx_done, tp_done = sem("zeroed"), sem("relx_done"), sem("tp_done")
        lv_done, st_loaded, pw_loaded, st_done = sem("lv_done"), sem("st_loaded"), sem("pw_loaded"), sem("st_done")
        z_done, wt_done, relu_done, iacc_done = sem("z_done"), sem("wt_done"), sem("relu_done"), sem("iacc_done")
        kidx_loaded = sem("kidx_loaded")
        kit_done, score_mm, srelu_done, sc_done = sem("kit_done"), sem("score_mm"), sem("srelu_done"), sem("sc_done")
        topk, masks_done = sem("topk_steps"), sem("masks_done")
        pool_chain = sem("pool_chain")
        ucx_done, d_done, qz_done = sem("ucx_done"), sem("d_done"), sem("qz_done")
        keys_padded = sem("keys_padded")
        tail_done, pm_done, kin_done, nat_done = sem("tail_done"), sem("pm_done"), sem("kin_done"), sem("nat_done")
        k_loaded = [[sem(f"k_loaded{b}_{hf}") for hf in range(2)] for b in range(2)]
        v_loaded = [sem(f"v_loaded{b}") for b in range(3)]
        keys_odd = sem("keys_odd_done")
        keys_done, logit_mm, lg_done, lgb_done = sem("keys_done"), sem("logit_mm"), sem("lg_done"), sem("lgb_done")
        slog_done, sexp_done, snorm_done = sem("slog_done"), sem("sexp_done"), sem("snorm_done")
        ptr_done, sout_mm, sout_done = sem("ptr_done"), sem("sout_mm"), sem("sout_done")
        own_done = sem("own_done")
        strip_loaded = sem("strip_loaded")
        plog_done, pexp_done, pnorm_done = sem("plog_done"), sem("pexp_done"), sem("pnorm_done")
        ppt_done, po_done = sem("ppt_done"), sem("po_done")
        cathi_done, cat_ready = sem("cathi_done"), sem("cat_ready")
        out_nat = [sem("out_nat0"), sem("out_nat1")]
        out_small, y_done = sem("out_small"), sem("y_done")
        s_y = [sem("out_y0"), sem("out_y1")]
        passed = {n: sem(f"passed_{n}") for n in ("sp", "act", "pool", "dve", "pe")}

        def hold(eng, who, s, v):
            eng.wait_ge(s, v)
            eng.sem_inc(passed[who], 1)

        def unit0(l, ph):
            return l * U_LAYER + (0, U_FFN, U_FFN + U_MIX)[ph]

        def tile0(l, ph):
            return l * T_LAYER + T_START + (0, T_FFN, T_FFN + T_MIX)[ph]

        def x0(l, ph):
            return l * X_LAYER + X_START + (0, 8 * FB, 8 * FB + 8, X_LAYER)[ph]

        def T(l, name):
            return tile0(l, 1) + MIX_NO[name] + 1

        def norm_no(l, ph):
            return l * 3 + ph

        TAIL = SEQ - 15
        NEWROWS = DB * DT
        rows_of = lambda t: P if t < 4 else NEWROWS
        CONV_TAPS, POOL_SC = 24, 30

        block = ctx.enter_context(nc.Block())

        @block.sync
        def _(sp):
            def load(l, ph, i, c, dst, src):
                hold(sp, "sp", units_split, unit0(l, ph) + 6 * i + c + 1)
                sp.dma_start(dst, src).then_inc(loaded[c % 3], 16)

            def k_rows(c):
                return raw[:, c % 3, :].rearrange("p (k n) -> p k n", k=KC)

            def index_pages(l, b, pgs):
                for pg in pgs:
                    page = sp.value_load(pt_sb[0:1, ds(b * NPG + pg, 1)], min_val=0, max_val=last_page)
                    sp.dma_start(kipages[:, ds(b, 1), pg, :].rearrange("p o d -> p (o d)"), a['cache_kidx'][l, page, :, :]).then_inc(kidx_loaded, 16)

            def ffn(l, f):
                ph = 2 * f
                gate, up = (a[f'ffn{f + 1}_{n}'].rearrange("l (k p) f -> l p k f", p=P) for n in ('gate', 'up'))
                down = a[f'ffn{f + 1}_down']

                def gate_up(i, j, c0):
                    for n, w in enumerate((gate, gate, up, up)):
                        load(l, ph, j, c0 + n, k_rows(c0 + n), w[l, :, :, ds(i * 256 + P * (n % 2), P)])

                def down_rows(i, j, c0):
                    for m in range(2):
                        load(l, ph, j, c0 + m, raw[:, (c0 + m) % 3, :], down[l, ds(i * 256 + m * P, P), :])

                gate_up(0, 0, 0)
                if f == 0:
                    with sp.Fori(0, DB) as j:
                        gate_up(j + 1, j, 4)
                        hold(sp, "sp", tiles, tile0(l, 0) + 1)
                        index_pages(l, j, range(0, NPG // 2))
                        down_rows(j, j, 8)
                        index_pages(l, j, range(NPG // 2, NPG))
                with sp.Fori(0 if f else DB, FB - 1) as j:
                    gate_up(j + 1, j, 4)
                    down_rows(j, j, 8)
                down_rows(FB - 1, 0, U_FFN - 2)

            def x_rows(t):
                if t >= 2:
                    sp.wait_ge(tiles, t - 1)
                src = (a['x_prompt'][0, t * P:(t + 1) * P, :] if t < 4
                       else a['x_sample'].rearrange("b t d -> (b t) d"))
                sp.dma_start(yst[0:rows_of(t), t % 2, :], src).then_inc(s_xrow[t % 2], 16)

            sp.dma_start(cst[:, :], a['consts']).then_inc(s_cst, 16)
            x_rows(0)
            x_rows(1)
            sp.dma_start(rel_sb[:, :], a['rel_bias']).then_inc(s_in, 16)
            sp.dma_start(pt_sb[0:1, :], a['page_table'].rearrange("(o b) n -> o (b n)", o=1)).then_inc(s_in, 16)
            for l in range(DEPTH):
                for n, v in enumerate(('norm_ffn1', 'norm_mix', 'norm_ffn2')):
                    sp.dma_start(vrows[l * 32 + 8 * n:l * 32 + 8 * n + 8, :],
                                 a[v][l, :].rearrange("(c p) -> c p", p=P)).then_inc(s_in, 16)
                sp.dma_start(vrows[l * 32 + 24:l * 32 + 30, :],
                             a['conv_w'][l, :, :].rearrange("j (c p) -> (j c) p", p=P)).then_inc(s_in, 16)
                sp.dma_start(vrows[l * 32 + 30:l * 32 + 32, :],
                             a['pool_scale'][l, :].rearrange("(c p) -> c p", p=P)).then_inc(s_in, 16)
            sp.dma_start(vrows[DEPTH * 32:DEPTH * 32 + 8, :],
                         a['norm_final'].rearrange("(c p) -> c p", p=P)).then_inc(s_in, 16)
            sp.dma_start(oh[:, :], a['onehots']).then_inc(s_oh, 16)
            for t in range(2, 5):
                x_rows(t)
            sp.dma_start(a['pool_sample'].rearrange("l b t c -> (l b) t c")[:, 0:11, :],
                         a['state_pool'].rearrange("l b t c -> (l b) t c")[:, DT:15, :]).then_inc(out_small, 16)

            w_in = a['w_in'].rearrange("l (k p) f -> l p k f", p=P)
            w_o = a['w_o'].rearrange("l (k p) f -> l p k f", p=P)
            ck, cv = (a[n].rearrange("l n p h d -> l n p (h d)") for n in ('cache_k', 'cache_v'))
            last_page = a['cache_k'].shape[1] - 1
            first_col = dict(QI=C_QI, CG=C_CG, XIN=C_XIN, BG=C_BG, U=C_U, Q=C_Q, K=C_K, V=C_V)

            def pages(l, b, pg0, n, dst, src, s):
                for pg in range(pg0, pg0 + n):
                    at_ = b * NPG + pg
                    page = sp.value_load(pt_sb[0:1, at_:at_ + 1], min_val=0, max_val=last_page)
                    sp.dma_start(dst[:, pg, :], src[l, page, :, :]).then_inc(s, 16)

            with sp.Fori(0, DEPTH) as l:
                ffn(l, 0)

                hold(sp, "sp", tiles, tile0(l, 0) + 1)
                sp.dma_start(srow[0:DB * 15, 0, :], a['state_pool'].rearrange("l b t c -> l (b t) c")[l, :, :]).then_inc(st_loaded, 16)
                sp.dma_start(srow[0:DB * 2, 1, :], a['state_conv'].rearrange("l b t c -> l (b t) c")[l, :, :]).then_inc(st_loaded, 16)
                for g in range(4):
                    r = 64 * (g % 2)
                    sp.dma_start(pw[r:r + 64, g // 2, r:r + 64], a['pool_w'][l, g, :, :]).then_inc(pw_loaded, 16)
                for c in range(4):
                    k0, s = 4 * (c % 2), raw[:, c % 3, 0:512].rearrange("p (k n) -> p k n", k=4)
                    if c < 2:
                        load(l, 1, 0, c, s[:, :, 0:ID], w_in[l, :, k0:k0 + 4, C_KI:C_KI + ID])
                        sp.dma_start(s[:, :, ID:2 * ID], w_in[l, :, k0:k0 + 4, C_KI:C_KI + ID]).then_inc(loaded[c % 3], 16)
                    else:
                        load(l, 1, 0, c, s, w_in[l, :, k0:k0 + 4, D_IN - P:D_IN])

                def z_unit(n):
                    f0 = first_col[Z_TILES[n][:-1]] + P * int(Z_TILES[n][-1])
                    load(l, 1, 0, n + 2, k_rows(n + 2), w_in[l, :, :, f0:f0 + P])

                for n in range(2, 6):
                    z_unit(n)
                for n in range(6, 26):
                    z_unit(n)

                def keys(b):
                    for hf in range(2):
                        hold(sp, "sp", tiles, T(l, f'KT{b - 2}_{2 * hf + 1}' if b >= 2 else 'V3'))
                        pages(l, b, 4 * hf, 4, kpages[b % 2], ck, k_loaded[b % 2][hf])

                for b in range(DB):
                    keys(b)
                hold(sp, "sp", kin_done, l * 2 + 2)
                sp.dma_start(a['kidx_prompt'].rearrange("l b (t p) d -> l p (b t) d", p=P)[l, :, :, :], ki_st[:, 0:4, :]).then_inc(out_small, 16)
                sp.dma_start(a['kidx_sample'].rearrange("l b t d -> l (b t) d")[l, :, :], ki_st[0:NEWROWS, 4, :]).then_inc(out_small, 16)
                for t in range(5):
                    hold(sp, "sp", nat_done, l * 10 + 2 * t + 2)
                    for n, rows in (('k', kn_stage[:, t, :] if t < 4 else kn_last[:, :]), ('v', vn[0:rows_of(t), t, :])):
                        dst = (a[n + '_prompt'].rearrange("l b s h d -> l (b s) (h d)")[l, t * P:(t + 1) * P, :] if t < 4
                               else a[n + '_sample'].rearrange("l b s h d -> l (b s) (h d)")[l, :, :])
                        sp.dma_start(dst, rows).then_inc(out_nat[t % 2], 16)
                hold(sp, "sp", tail_done, l * 6 + 6)
                sp.dma_start(a['pool_prompt'].rearrange("l b t (j c) -> l (b t) j c", c=P)[l, :, :, :], tail_st[0:15, :, :]).then_inc(out_small, 16)
                for t in range(DT):
                    sp.dma_start(a['pool_sample'].rearrange("l b t (j c) -> l b t j c", c=P)[l, :, 11 + t, :, :],
                                 tail_st[15 + t:15 + t + 4 * DB - 3:4, :, :]).then_inc(out_small, 16)
                for t in range(2):
                    sp.dma_start(a['conv_sample'].rearrange("l b t (j c) -> l b t j c", c=P)[l, :, t, :, :],
                                 conv_st[4 + t:4 + t + 6 * DB - 5:6, :, 0:P]).then_inc(out_small, 16)
                sp.dma_start(a['conv_prompt'].rearrange("l b t (j c) -> l (b t) j c", c=P)[l, :, :, :], conv_st[0:2, :, P:2 * P]).then_inc(out_small, 16)
                pages(l, 0, 0, NPG, vpages[0], cv, v_loaded[0])
                hold(sp, "sp", s_scr, 16)
                hold(sp, "sp", tiles, T(l, f'KT{DB - 2}_3'))
                for h in range(NH):
                    src = bass.AP(a['scratch'].tensor, h * P * NTP + P - 1, [[NTP - 1, P], [1, SEQ]])
                    sp.dma_start(strip[:, h, :], src).then_inc(strip_loaded, 16)
                for b in range(1, DB):
                    if b == 1:
                        hold(sp, "sp", tiles, T(l, f'KT{DB - 1}_3'))
                    elif b == 2:
                        hold(sp, "sp", logit_mm, (l + 1) * 3 * DB)
                    else:
                        hold(sp, "sp", sout_mm, l * DB + b - 2)
                    pages(l, b, 0, NPG, vpages[b % 3], cv, v_loaded[b % 3])
                hold(sp, "sp", tiles, T(l, 'PTN1'))
                for n in range(8):
                    load(l, 1, 0, 28 + n, k_rows(28 + n), w_o[l, :, :, n * P:(n + 1) * P])
                ffn(l, 1)

            for t in range(5):
                sp.wait_ge(y_done, t + 1)
                dst = (a['y_prompt'][0, t * P:(t + 1) * P, :] if t < 4 else a['y_sample'].rearrange("b t d -> (b t) d"))
                sp.dma_start(dst, yst[0:rows_of(t), t % 2, :]).then_inc(s_y[t % 2], 16)
            sp.wait_ge(s_y[0], 48)
            sp.wait_ge(s_y[1], 32)
            sp.wait_ge(out_nat[0], DEPTH * 96)
            sp.wait_ge(out_nat[1], DEPTH * 64)
            sp.wait_ge(out_small, 16 + DEPTH * 16 * OUT_SMALL)

        @block.scalar
        def _(act):
            def raw_loads(l, ph, i, c):
                twice = 16 if c % 3 < 2 else 0
                before = (0, U_FFN, U_FFN + U_MIX)[ph] // 3
                return l * (16 * (U_LAYER // 3) + twice) + 32 * i + 16 * (before + c // 3 + 1) + (twice if ph else 0)

            def hi(l, ph, i, c, n=1024, slot_free=None):
                if slot_free is not None:
                    act.wait_ge(tiles, slot_free)
                act.wait_ge(loaded[c % 3], raw_loads(l, ph, i, c))
                act.activation(w_hi[:, c % 6, 0:n], raw[:, c % 3, 0:n], ACT.Copy).then_inc(units_hi, 1)

            AHEAD = 3

            def squares(k, xready, early=True, ahead=None):
                for c in range(KC):
                    act.wait_ge(x_updates, xready - (KC - 1 - c if early else 0))
                    if c >= 3:
                        act.wait_ge(ssum_done, k * (KC - 1) + c - 2)
                    slot = 1 + c % 2 if c else 0
                    act.activation(sq[:, slot, :], xT[:, c, :], ACT.Square).then_inc(sq_done, 1)
                    if ahead is not None and 4 <= c < 4 + AHEAD:
                        hi(ahead[0], ahead[1], 0, c - 4, ahead[2])

            def root(stats_done):
                act.wait_ge(tiles, stats_done)
                act.activation(rtok[:, :], ps[:, 0, 0:5], ACT.Sqrt, scale=1.0 / D, bias=epsb[:, 0:1]).then_inc(rt_done, 1)

            def split_h(l, ph):
                for c in range(KC):
                    act.wait_ge(normed_done, norm_no(l, ph) * KC + c + 1)
                    act.activation(h_hi[:, c, :], normed[:, c % 4, :], ACT.Copy,
                                   scale=lv[:, 8 * ph + c:8 * ph + c + 1]).then_inc(hhi_done, 1)
                    if c % 2:
                        act.activation(normed[:, c % 4, :], normed[:, c % 4, :], ACT.Copy,
                                       scale=lv[:, 8 * ph + c:8 * ph + c + 1]).then_inc(gained, 1)

            def ffn(l, f):
                ph = 2 * f
                t0, s0 = tile0(l, ph), (l * 2 + f) * 2 * FB
                root(t0 + 1)
                if f == 0:
                    hi(l, ph, 0, 0)
                    hi(l, ph, 0, 1)
                split_h(l, ph)

                def silu_of(m, tile):
                    act.wait_ge(tiles, tile)
                    act.activation(halves(silu[:, m, :]), pair(m), ACT.Silu).then_inc(silu_done, 1)

                def act_high(i, down_done):
                    act.wait_ge(tiles, down_done)
                    for m in range(2):
                        act.wait_ge(gu_done, s0 + 2 * i + m + 1)
                        act.activation(act_hi[:, m, :], gated[:, m, :], ACT.Copy).then_inc(acthi_done, 1)

                for c in range(4):
                    if f == 0 or c + 2 >= AHEAD:
                        hi(l, ph, 0, c + 2)
                    if c < 2:
                        silu_of(c, t0 + 2 + c)
                act_high(0, t0 + 1)
                with act.Fori(0, FB - 1) as j:
                    for c in range(4, 10):
                        hi(l, ph, j, c + 2, slot_free=t0 + 12 * j + (-4, -3, 5, 5, 6, 7)[c - 4])
                        if c < 6:
                            act.wait_ge(gu_done, s0 + 2 * j + c - 3)
                            silu_of(c - 4, t0 + 12 * j + c + 2)
                    act_high(j + 1, t0 + 12 * j + 17)
                squares(norm_no(l, ph + 1), x0(l, ph + 1), ahead=None if f else (l, 1, 512))

            squares(0, X_START, early=False)
            act.wait_ge(tiles, 7)
            act.activation(tp_sb[:, 0:512], ps[0:NH, 4, :], ACT.Copy).then_inc(tp_done, 1)
            act.activation(tp_sb[:, 512:NTP], ps[0:NH, 5, 0:NTP - 512], ACT.Copy).then_inc(tp_done, 1)
            act.wait_ge(tp_done, 2)
            act.dma_start(a['scratch'], tp_sb[:, :].unsqueeze(1).to_broadcast([NH, P, NTP])).then_inc(s_scr, 16)
            act.wait_ge(zeroed, 4)
            act.wait_ge(tiles, T_START)

            with act.Fori(0, DEPTH) as l:
                act.wait_ge(lv_done, l + 1)
                ffn(l, 0)
                root(T(l, 'STATS'))
                hi(l, 1, 0, 3, 512)
                act.wait_ge(tiles, T(l, 'ST'))
                act.activation(states[:, :, :], ps[:, 2:4, 0:136], ACT.Copy).then_inc(st_done, 1)
                split_h(l, 1)
                zdst = {'KI': ki[:, :], 'WI': wi[:, :]}
                for c in range(4):
                    zdst |= {f'QI{c}': qi[:, c, :], f'Q{c}': qT[:, c, :], f'K{c}': kT[:, c, :], f'V{c}': v_sb[:, c, :]}
                for j in range(2):
                    zdst |= {n + str(j): cz[:, q, :] for q, n in enumerate(('CG', 'XIN', 'BG', 'U'))}

                def z(name):
                    act.wait_ge(tiles, T(l, name))
                    act.activation(halves(zdst[name]), pair((Z_NO[name] + 2) % 4), ACT.Copy).then_inc(z_done, 1)

                def hi_m(c):
                    prev = c - 6
                    name = ('KI' if prev < 2 else Z_TILES[max(prev - 2, 1)] if prev < 28 else f'WO{prev - 28}')
                    hi(l, 1, 0, c, slot_free=T(l, name))

                def z_with_hi(first, last, ahead=4):
                    for n in range(first, last):
                        if n + ahead < 6:
                            hi(l, 1, 0, n + ahead)
                        else:
                            hi_m(n + ahead)
                        z(Z_TILES[n])

                z_with_hi(0, 6)
                for n in range(12):
                    L = (2 + n // 4) * P
                    act.wait_ge(tiles, T(l, f'IS{n}'))
                    if n >= 2:
                        act.wait_ge(iacc_done, l * 27 + 2 * (n - 1))
                    act.activation(prelu[:, n % 2, :, 0:L], pair(2 + n % 2, P, L), ACT.Relu, scale=ID ** -0.5).then_inc(relu_done, 1)
                hold(act, "act", wt_done, l * 6 + 6)
                for b in range(DB):
                    act.wait_ge(tiles, T(l, f'KIT{b}'))
                    if b >= 2:
                        hold(act, "act", score_mm, l * DB + b - 1)
                    act.activation(kidxT[:, b % 2, 0:PAST].rearrange("p (a b) -> p a b", a=2), pair(2 + b % 2, ID, 512), ACT.Copy).then_inc(kit_done, 1)
                    act.activation(kidxT[:, b % 2, PAST:PAST + DT], ki[0:ID, SEQ + DT * b:SEQ + DT * (b + 1)], ACT.Copy).then_inc(kit_done, 1)
                    if b == 4:
                        act.wait_ge(score_mm, l * DB + 4)
                        act.activation(srelu[:, 0, :, :], ps[:, 0:3, 0:LT], ACT.Relu, scale=ID ** -0.5).then_inc(srelu_done, 1)
                act.wait_ge(score_mm, l * DB + DB)
                act.activation(srelu[:, 1, :, :], ps[:, 0:3, 0:LT], ACT.Relu, scale=ID ** -0.5).then_inc(srelu_done, 1)
                act.wait_ge(tiles, T(l, 'SC'))
                act.activation(work_s[:, :].rearrange("p (a b) -> p a b", a=3), ps[0:32, 4:7, 0:LT], ACT.Copy).then_inc(sc_done, 1)

                def tail_and_pooled(j):
                    act.wait_ge(tiles, T(l, f'TL{j}'))
                    act.activation(tail_st[:, j, :], ps[0:47, 0, 0:P], ACT.Copy).then_inc(tail_done, 1)
                    act.activation(conv_st[:, j, 0:P], ps[0:6 * DB, 1, 0:P], ACT.Copy).then_inc(tail_done, 1)
                    act.activation(conv_st[0:2, j, P:2 * P], ps[0:2, 1, P:2 * P], ACT.Copy).then_inc(tail_done, 1)
                    act.wait_ge(tiles, T(l, f'PM{j}'))
                    act.activation(halves(cat[:, 2 + j, :]), pair(1), ACT.Copy, scale=lv[:, POOL_SC + j:POOL_SC + j + 1]).then_inc(pm_done, 1)

                z_with_hi(6, 18)
                hi_m(22)
                hi_m(23)
                act.wait_ge(iacc_done, l * 27 + 24)
                tail_and_pooled(0)
                for n in range(18, 26):
                    if n < 22:
                        hi_m(n + 6)
                    z(Z_TILES[n])
                act.wait_ge(tiles, T(l, 'KIN'))
                act.activation(ki_st[:, 0:4, :], ps[:, 0, 0:4 * ID].rearrange("p (t d) -> p t d", d=ID), ACT.Copy).then_inc(kin_done, 1)
                act.activation(ki_st[0:NEWROWS, 4, :], ps[0:NEWROWS, 0, 4 * ID:5 * ID], ACT.Copy).then_inc(kin_done, 1)
                for t in range(5):
                    act.wait_ge(tiles, T(l, f'NT{t}'))
                    bank = 2 * ((t + 1) % 4)
                    act.activation(kn_stage[:, t, :] if t < 4 else kn_last[:, :], ps[0:rows_of(t), bank, :], ACT.Copy).then_inc(nat_done, 1)
                    act.activation(vn[0:rows_of(t), t, :], ps[0:rows_of(t), bank + 1, :], ACT.Copy).then_inc(nat_done, 1)
                for b in range(DB):
                    for j in (0, 2):
                        act.wait_ge(tiles, T(l, f'KT{b}_{j}'))
                        if b > 0:
                            hold(act, "act", logit_mm, l * 3 * DB + 3 * b - (2 if j == 0 else 0))
                        act.activation(keysT[:, :, 256 * j:256 * j + 256], ps[:, 4:6, :].rearrange("p a (c n) -> p (a c) n", n=256),
                                       ACT.Copy).then_inc(keys_done, 1)
                    act.activation(keysT[:, :, PAST:PAST + DT], kT[:, :, SEQ + DT * b:SEQ + DT * (b + 1)], ACT.Copy).then_inc(keys_done, 1)
                    if b % 4 == 3:
                        act.wait_ge(logit_mm, l * 3 * DB + 3 * b + 3)
                        act.activation(lg[:, b // 4, :].rearrange("p (a b) -> p a b", a=3), ps[:, 0:3, 0:LT], ACT.Copy, scale=SCALE).then_inc(lg_done, 1)
                    if b == 3:
                        tail_and_pooled(1)
                for g in range(2):
                    act.wait_ge(slog_done, l * 4 + 2 * g + 2)
                    act.activation(lg[:, g, :], lg[:, g, :], ACT.Exp, bias=sstat[:, g, 1:2], accum_out=sstat[:, g, 2:3]).then_inc(sexp_done, 1)

                for n in range(18):
                    if n < 16:
                        L = (n // 4 + 1) * P
                        act.wait_ge(plog_done, l * 64 + 4 * n + 4)
                        for e in range(2):
                            act.activation(probs[:, n % 2, e, 0:L], probs[:, n % 2, e, 0:L], ACT.Exp,
                                           bias=stat[:, n % 2, 2 + e:3 + e], accum_out=stat[:, n % 2, 4 + e:5 + e]).then_inc(pexp_done, 1)
                    if n >= 2:
                        m = n - 2
                        act.wait_ge(tiles, T(l, f'PO{m}'))
                        act.activation(cat[:, 4 + m % 4, P * (m // 4):P * (m // 4) + P], ps[:, 6, 0:P], ACT.Copy).then_inc(po_done, 1)
                    if 1 <= n < 17:
                        L = ((n - 1) // 4 + 1) * P
                        act.wait_ge(tiles, T(l, f'PT{n - 1}'))
                        if n >= 2:
                            act.wait_ge(tiles, T(l, f'PO{n - 2}'))
                        act.activation(pTp[:, :, 0:L], pair(2, P, L), ACT.Copy).then_inc(ppt_done, 1)
                    if n == 16:
                        act.wait_ge(d_done, l * 2 + 2)
                        for c in range(4):
                            act.activation(h_hi[:, c, :], cat[:, c, :], ACT.Copy).then_inc(cathi_done, 1)
                        act.wait_ge(sout_mm, (l + 1) * DB)
                        for c in range(28, 31):
                            hi_m(c)

                act.wait_ge(sout_done, l * 2 + 2)
                act.wait_ge(po_done, (l + 1) * 16)
                for c in range(4, KC):
                    act.activation(h_hi[:, c, :], cat[:, c, :], ACT.Copy).then_inc(cathi_done, 1)
                for n in range(3, 8):
                    hi_m(28 + n)
                squares(norm_no(l, 2), x0(l, 2), ahead=(l, 2, 1024))
                ffn(l, 1)

            root(T_START + DEPTH * T_LAYER + 1)
            for c in range(KC):
                act.wait_ge(normed_done, 3 * DEPTH * KC + c + 1)
                act.activation(yT[:, c, :], normed[:, c % 4, :], ACT.Copy, scale=vecs[:, DEPTH * 32 + c:DEPTH * 32 + c + 1]).then_inc(hhi_done, 1)
            for t in range(5):
                act.wait_ge(tiles, T_START + DEPTH * T_LAYER + 2 + t)
                if t >= 2:
                    act.wait_ge(s_y[t % 2], 16 * (t // 2))
                b0 = 2 * (t % 4)
                act.activation(yst[0:rows_of(t), t % 2, :].rearrange("p (a b) -> p a b", a=2), ps[0:rows_of(t), b0:b0 + 2, :], ACT.Copy).then_inc(y_done, 1)

        @block.gpsimd
        def _(pool):
            def lo(l, ph, i, c, n=1024):
                hold(pool, "pool", units_hi, unit0(l, ph) + 6 * i + c + 1)
                pool.tensor_tensor(w_lo[:, c % 6, 0:n], raw[:, c % 3, 0:n], w_hi[:, c % 6, 0:n].bitcast(F32), ALU.subtract).then_inc(units_split, 1)

            def low_odd(l, ph):
                k = norm_no(l, ph)
                for c in range(1, KC, 2):
                    hold(pool, "pool", gained, k * (KC // 2) + c // 2 + 1)
                    pool.tensor_tensor(h_lo[:, c, :], normed[:, c % 4, :], h_hi[:, c, :].bitcast(F32), ALU.subtract).then_inc(h_odd, 1)

            def ffn(l, ph):
                for c in range(4):
                    if c == 2:
                        low_odd(l, ph)
                    lo(l, ph, 0, c)
                with pool.Fori(0, FB - 1) as j:
                    for c in range(4, 10):
                        lo(l, ph, j, c)
                for c in range(U_FFN - 2, U_FFN):
                    lo(l, ph, 0, c)

            pool.memset(pw[:, :, :], 0.0).then_inc(zeroed, 1)
            pool.wait_ge(tiles, T_START)
            pool.sem_inc(units_split, RAW_SLOTS)

            with pool.Fori(0, DEPTH) as l:
                ffn(l, 0)
                steps = [0]

                def link(ins):
                    steps[0] += 1
                    ins.then_inc(pool_chain, 1)
                    hold(pool, "pool", pool_chain, l * POOL_CHAIN + steps[0])

                new = lambda t, w: t.rearrange("p (b s) -> p b s", s=w)
                ucx_new, ext_new = new(ucx[:, 2 + SEQ:NUX], 6), new(pb[0][:, 15 + SEQ:NPX], 19)

                def conv_products(j):
                    hold(pool, "pool", z_done, l * 26 + (10, 22)[j])
                    hold(pool, "pool", st_done, l + 1)
                    if j == 1:
                        hold(pool, "pool", tiles, T(l, 'TL0'))
                    link(pool.memset(ucx[:, 0:2], 0.0))
                    link(pool.tensor_copy(ucx_new[:, :, 0:2], new(states[:, j, 120:136], 2)))
                    link(pool.tensor_tensor(ucx[:, 2:2 + SEQ], cz[:, 0, 0:SEQ], cz[:, 1, 0:SEQ], ALU.mult))
                    pool.tensor_tensor(ucx_new[:, :, 2:6], new(cz[:, 0, SEQ:TOK], DT), new(cz[:, 1, SEQ:TOK], DT), ALU.mult).then_inc(ucx_done, 1)
                    hold(pool, "pool", ucx_done, l * 2 + j + 1)

                def conv_sum(j, part):
                    n = NUX - 2
                    t0, t1 = (t[:, 0:n] for t in conv_t)
                    tap = lambda q: lv[:, CONV_TAPS + 2 * q + j:CONV_TAPS + 2 * q + j + 1]
                    if part == 1:
                        link(pool.tensor_tensor(t0, t0, t1, ALU.add))
                        link(pool.tensor_tensor(cat[:, j, 0:SEQ], t0[:, 0:SEQ], cz[:, 2, 0:SEQ], ALU.mult))
                        link(pool.tensor_tensor(new(cat[:, j, SEQ:TOK], DT), new(conv_t[0][:, SEQ + 2:NUX], 6)[:, :, 0:DT],
                                                new(cz[:, 2, SEQ:TOK], DT), ALU.mult))
                        return
                    hold(pool, "pool", s_scr, 16)
                    link(pool.tensor_scalar(t0, ucx[:, 0:n], tap(0), None, ALU.mult))
                    link(pool.tensor_scalar(t1, ucx[:, 1:n + 1], tap(1), None, ALU.mult))
                    link(pool.tensor_tensor(t0, t0, t1, ALU.add))
                    link(pool.tensor_scalar(t1, ucx[:, 2:n + 2], tap(2), None, ALU.mult))

                def windows(j, part):
                    u, (e, s, w) = cz[:, 3, :], pb
                    if part == 1:
                        if j == 0:
                            link(pool.tensor_tensor(w[64:P, 3:NPX], s[64:P, 3:NPX], s[64:P, 1:NPX - 2], ALU.add))
                        else:
                            link(pool.tensor_tensor(w[:, 3:NPX], s[:, 3:NPX], s[:, 1:NPX - 2], ALU.add))
                            link(pool.tensor_tensor(s[:, 7:NPX], w[:, 7:NPX], w[:, 3:NPX - 4], ALU.add))
                            link(pool.tensor_tensor(w[64:P, 15:NPX], s[64:P, 15:NPX], s[64:P, 7:NPX - 8], ALU.add))
                        link(pool.tensor_copy(w[0:64, 15:NPX], s[0:64, 15:NPX]))
                        return
                    link(pool.memset(e[:, 0:15], 0.0))
                    link(pool.tensor_copy(ext_new[:, :, 0:15], new(states[:, j, 0:120], 15)))
                    link(pool.tensor_copy(e[:, 15:15 + SEQ], u[:, 0:SEQ]))
                    link(pool.tensor_copy(ext_new[:, :, 15:19], new(u[:, SEQ:TOK], DT)))
                    link(pool.tensor_tensor(s[:, 1:NPX], e[:, 1:NPX], e[:, 0:NPX - 1], ALU.add))

                def pool_diff(j):
                    u, (d, m, w) = cz[:, 3, :], pb
                    link(pool.tensor_scalar(m[:, 15:NPX], w[:, 15:NPX], cst[:, CO['rwin'] + j:CO['rwin'] + j + 1], None, ALU.mult))
                    link(pool.tensor_tensor(m[:, 15:31], w[:, 15:31], cst[:, CO['rcnt'] + 16 * j:CO['rcnt'] + 16 * j + 16], ALU.mult))
                    link(pool.tensor_tensor(d[:, 0:SEQ], m[:, 15:15 + SEQ], u[:, 0:SEQ], ALU.subtract))
                    pool.tensor_tensor(new(d[:, SEQ:TOK], DT), new(m[:, 15 + SEQ:NPX], 19)[:, :, 15:19], new(u[:, SEQ:TOK], DT), ALU.subtract).then_inc(d_done, 1)
                    hold(pool, "pool", d_done, l * 2 + j + 1)

                for c in range(14):
                    if c == 4:
                        low_odd(l, 1)
                    lo(l, 1, 0, c, 512 if c < 4 else 1024)
                conv_products(0)
                lo(l, 1, 0, 14)
                conv_sum(0, 0)
                lo(l, 1, 0, 15)
                conv_sum(0, 1)
                lo(l, 1, 0, 16)
                windows(0, 0)
                lo(l, 1, 0, 17)
                hold(pool, "pool", units_split, unit0(l, 1) + 18 + RAW_SLOTS)
                windows(0, 1)
                lo(l, 1, 0, 18)
                pool_diff(0)
                lo(l, 1, 0, 19)
                for c in range(20, 28):
                    lo(l, 1, 0, c)
                hold(pool, "pool", units_split, unit0(l, 1) + 28 + RAW_SLOTS)
                conv_products(1)
                hold(pool, "pool", z_done, l * 26 + 14)
                hold(pool, "pool", tiles, T(l, 'SC'))
                link(pool.memset(qz[:, :, :, :], 0.0))
                for h in range(NH):
                    r = 64 * (h % 2)
                    ins = pool.tensor_copy(qz[r:r + 64, h // 2, :, DT * h:DT * (h + 1)], new(qT[r:r + 64, h // 2, SEQ:TOK], DT))
                    ins.then_inc(qz_done, 1)
                hold(pool, "pool", qz_done, (l + 1) * NH)
                hold(pool, "pool", tiles, T(l, 'V3'))
                pool.memset(keysT[:, :, PAST + DT:LS], 0.0).then_inc(keys_padded, 1)
                hold(pool, "pool", keys_padded, l + 1)
                hold(pool, "pool", tiles, T(l, 'PM0'))
                for part in range(2):
                    conv_sum(1, part)
                for part in range(2):
                    windows(1, part)
                pool_diff(1)
                for g in range(2):
                    hold(pool, "pool", lg_done, l * 2 + g + 1)
                    pool.tensor_tensor(lg[:, g, :], lg[:, g, :], bias_s[:, :], ALU.add).then_inc(lgb_done, 1)
                for c in range(28, 36):
                    lo(l, 1, 0, c)
                assert steps[0] == POOL_CHAIN, steps
                ffn(l, 2)

        @block.vector
        def _(dve):
            def add_square(k, c):
                dve.wait_ge(sq_done, k * KC + c + 1)
                if c > 1:
                    dve.wait_ge(ssum_done, k * (KC - 1) + c - 1)
                dve.tensor_tensor(sq[:, 0, :], sq[:, 0, :], sq[:, 1 + c % 2, :], ALU.add).then_inc(ssum_done, 1)

            def norm(l, k):
                dve.wait_ge(rt_done, k + 1)
                dve.reciprocal(rtok[:, :], rtok[:, :]).then_inc(rms_done, 1)
                dve.wait_ge(rms_done, 2 * k + 1)
                dve.tensor_tensor(rdiag[:, :, :], ident.unsqueeze(1).to_broadcast([P, 5, P]), rtok[:, :].unsqueeze(2).to_broadcast([P, 5, P]),
                                  ALU.mult).then_inc(rms_done, 1)
                over_rms = pair(0 if l is not None and l[1] == 1 else 3)
                dve.wait_ge(rb_done, k + 1)
                for c in range(KC):
                    if c >= 4:
                        if l is None:
                            dve.wait_ge(hhi_done, k * KC + c - 3)
                        else:
                            dve.wait_ge(h_odd if c % 2 else h_ready, k * (KC // 2) + c // 2 - 1)
                    dve.tensor_tensor(halves(normed[:, c % 4, :]), halves(xT[:, c, :]), over_rms, ALU.mult).then_inc(normed_done, 1)
                    if c % 2 and l is not None:
                        low(l[0], l[1], k, c - 1)

            def low(l, ph, k, c):
                dve.wait_ge(hhi_done, k * KC + c + 1)
                dve.scalar_tensor_tensor(h_lo[:, c, :], normed[:, c % 4, :], lv[:, 8 * ph + c:8 * ph + c + 1],
                                         h_hi[:, c, :].bitcast(F32), ALU.mult, ALU.subtract).then_inc(h_ready, 1)

            def ffn(l, f):
                ph = 2 * f
                t0, s0, xb = tile0(l, ph), (l * 2 + f) * 2 * FB, x0(l, ph)
                norm((l, ph), norm_no(l, ph))

                def gate_up(i, tile, again):
                    for m in range(2):
                        dve.wait_ge(silu_done, s0 + 2 * i + m + 1)
                        if again:
                            dve.wait_ge(act_ready, s0 + 2 * i + m - 1)
                        dve.wait_ge(tiles, tile + m)
                        dve.tensor_tensor(halves(gated[:, m, :]), pair(2 + m), halves(silu[:, m, :]), ALU.mult).then_inc(gu_done, 1)

                def act_low(i):
                    for m in range(2):
                        dve.wait_ge(acthi_done, s0 + 2 * i + m + 1)
                        dve.tensor_tensor(act_lo[:, m, :], gated[:, m, :], act_hi[:, m, :].bitcast(F32), ALU.subtract).then_inc(act_ready, 1)

                def add_down(i, tile, last=False):
                    for c in range(KC):
                        dve.wait_ge(x_updates, xb + 8 * i)
                        dve.wait_ge(tiles, tile + c)
                        dve.scalar_tensor_tensor(halves(xT[:, c, :]), pair(c % 4), 0.5, halves(xT[:, c, :]), ALU.mult, ALU.add).then_inc(x_updates, 1)
                        if last and c >= 2:
                            add_square(norm_no(l, ph + 1), c - 1)
                    if last:
                        add_square(norm_no(l, ph + 1), KC - 1)

                gate_up(0, t0 + 4, False)
                act_low(0)
                with dve.Fori(0, FB - 1) as j:
                    gate_up(j + 1, t0 + 12 * j + 8, True)
                    add_down(j, t0 + 12 * j + 10)
                    act_low(j + 1)
                add_down(FB - 1, t0 + T_FFN - 7, last=True)

            dve.memset(epsb[:, :], EPS).then_inc(zeroed, 1)
            dve.memset(relx[:, :, :], 0.0).then_inc(relx_done, 1)
            dve.wait_ge(s_in, 16 * S_IN)
            dve.wait_ge(relx_done, 1)
            for t in range(DT):
                for b in range(4):
                    dve.tensor_copy(relx[:, t, :].rearrange("p (b h t) -> p b h t", b=4, h=NH)[:, b, :, t], rel_sb[:, :]).then_inc(relx_done, 1)
            for t in range(5):
                dve.wait_ge(tiles, t + 1)
                r = rows_of(t)
                dve.tensor_copy(xT[:, :, t * P:t * P + r].rearrange("p (a c) n -> p a c n", a=2),
                                ps[:, 2 * (t % 4):2 * (t % 4) + 2, :].rearrange("p a (c n) -> p a c n", n=P)[:, :, :, 0:r]).then_inc(x_updates, 1)
            dve.wait_ge(tiles, 6)
            dve.tensor_copy(vecs[:, :], ps[:, 2, 0:DEPTH * 32 + 8]).then_inc(zeroed, 1)
            for c in range(1, KC):
                add_square(0, c)
            dve.wait_ge(tiles, 8)
            dve.tensor_copy(bias_s[:, :].rearrange("p (a b) -> p a b", a=3), ps[:, 0:3, 0:LT]).then_inc(zeroed, 1)
            dve.sem_inc(topk, 3)
            dve.wait_ge(zeroed, 4)

            with dve.Fori(0, DEPTH) as l:
                dve.tensor_copy(lv[:, :], vecs[:, ds(l * 32, 32)]).then_inc(lv_done, 1)
                hold(dve, "dve", lv_done, l + 1)
                ffn(l, 0)
                norm((l, 1), norm_no(l, 1))
                dve.wait_ge(tiles, T(l, 'WT'))
                dve.tensor_scalar(wi_nat[:, :, :], ps[:, 0, 0:4 * P].rearrange("p (t r) -> p t r", t=4)[:, :, P - IH:P], IH ** -0.5, None, ALU.mult).then_inc(wt_done, 1)
                for g in range(2):
                    dve.tensor_tensor(wsel[:, g, :], ps[:, 1, 0:32], C('own_query', n=32, off=32 * g), ALU.mult).then_inc(wt_done, 1)
                q4 = qis[:, :, :].rearrange("p b (c e t) -> p b c e t", e=2, t=DT)
                for e in range(2):
                    for c in range(4):
                        src = (qi[0:ID, c, SEQ:TOK] if e == 0 else ps[0:ID, 1, 32 * (c + 1):32 * (c + 2)])
                        last = dve.tensor_copy(q4[:, :, c, e, :], src.rearrange("p (b t) -> p b t", t=DT))
                        if c == 3:
                            last.then_inc(wt_done, 1)
                dve.memset(kidxT[:, :, PAST + DT:LS], 0.0).then_inc(wt_done, 1)
                dve.wait_ge(wt_done, l * 6 + 6)
                for n in range(12):
                    qb, c = 1 + n // 4, n % 4
                    L = (qb + 1) * P
                    work = work_p[:, WOFF[qb]:WOFF[qb] + L]
                    for e in range(2):
                        w = wi_nat[:, qb, 2 * c + e:2 * c + e + 1]
                        dve.wait_ge(relu_done, l * 12 + n + 1)
                        if c == e == 0:
                            dve.tensor_scalar(work, prelu[:, n % 2, e, 0:L], w, None, ALU.mult).then_inc(iacc_done, 1)
                        else:
                            dve.wait_ge(iacc_done, l * 27 + 2 * n + e)
                            dve.scalar_tensor_tensor(work, prelu[:, n % 2, e, 0:L], w, work, ALU.mult, ALU.add).then_inc(iacc_done, 1)
                dve.wait_ge(iacc_done, l * 27 + 24)
                for qb in range(1, QB):
                    diag = work_p[:, WOFF[qb] + qb * P:WOFF[qb] + (qb + 1) * P]
                    dve.tensor_tensor(diag, diag, C('causal'), ALU.add).then_inc(iacc_done, 1)
                hold(dve, "dve", iacc_done, l * 27 + 27)
                with dve.Fori(0, TOPK_P // 8) as r:
                    for n in range(6):
                        qb = 1 + n % 3
                        work = work_p[:, WOFF[qb]:WOFF[qb] + (qb + 1) * P]
                        hold(dve, "dve", topk, l * TOPK_STEPS + r * 6 + n + 1)
                        if n < 3:
                            dve.max(top8[:, n, :], work).then_inc(topk, 1)
                        else:
                            dve.match_replace(work, top8[:, n - 3, :], work, TAKEN).then_inc(topk, 1)
                hold(dve, "dve", sc_done, l + 1)
                dve.tensor_tensor(work_s[:, PAST:LS], work_s[:, PAST:LS], C('causal_new', 32), ALU.add).then_inc(masks_done, 1)
                hold(dve, "dve", masks_done, l * 3 + 1)
                with dve.Fori(0, TOPK_S // 8) as r:
                    hold(dve, "dve", topk, l * TOPK_STEPS + 96 + r * 2 + 3)
                    dve.max(top8[0:32, 0, :], work_s[:, :]).then_inc(topk, 1)
                    hold(dve, "dve", topk, l * TOPK_STEPS + 96 + r * 2 + 4)
                    dve.match_replace(work_s[:, :], top8[0:32, 0, :], work_s[:, :], TAKEN).then_inc(topk, 1)
                hold(dve, "dve", topk, (l + 1) * TOPK_STEPS + 3)
                for work in (work_s, work_p):
                    dve.tensor_scalar(work[:, :], work[:, :], TAKEN / 2, NEG, ALU.is_gt, ALU.mult).then_inc(masks_done, 1)

                for b in range(DB):
                    for j in (1, 3):
                        dve.wait_ge(tiles, T(l, f'KT{b}_{j}'))
                        if b > 0:
                            dve.wait_ge(logit_mm, l * 3 * DB + 3 * b - (1 if j == 1 else 0))
                        dve.tensor_copy(keysT[:, :, 256 * j:256 * j + 256], ps[:, 6:8, :].rearrange("p a (c n) -> p (a c) n", n=256)).then_inc(keys_odd, 1)

                def s_logits(g):
                    b0 = (4, 0)[g]
                    hold(dve, "dve", lgb_done, l * 2 + g + 1)
                    hold(dve, "dve", tiles, T(l, f'MX{g}'))
                    row = lg[:, g, :].rearrange("p (a b) -> p a b", a=3)
                    dve.tensor_tensor_reduce(out=row, in0=ps[:, b0:b0 + 3, 0:LT], in1=row, scale=1.0, scalar=2 * NEG, op0=ALU.add, op1=ALU.max,
                                             accum_out=sstat[:, g, 0:1]).then_inc(slog_done, 1)
                    dve.wait_ge(slog_done, l * 4 + 2 * g + 1)
                    dve.tensor_scalar(sstat[:, g, 1:2], sstat[:, g, 0:1], -1.0, None, ALU.mult).then_inc(slog_done, 1)

                def s_norm(g):
                    n0 = l * 6 + 3 * g
                    dve.wait_ge(sexp_done, l * 2 + g + 1)
                    dve.reciprocal(sstat[:, g, 3:4], sstat[:, g, 2:3]).then_inc(snorm_done, 1)
                    dve.wait_ge(snorm_done, n0 + 1)
                    dve.tensor_scalar(lg[:, g, :], lg[:, g, :], sstat[:, g, 3:4], None, ALU.mult).then_inc(snorm_done, 1)
                    dve.wait_ge(snorm_done, n0 + 2)
                    if g == 1:
                        dve.wait_ge(tiles, T(l, 'PTN0'))
                    new_p = lg[:, g, PAST:PAST + DT].unsqueeze(1).to_broadcast([P, DB, DT])
                    dve.tensor_tensor(pnew[:, :].rearrange("p (b t) -> p b t", t=DT), new_p,
                                      C('own_batch', n=32, off=32 * g).rearrange("p (b t) -> p b t", t=DT), ALU.mult).then_inc(snorm_done, 1)

                def s_transposed(g):
                    dve.wait_ge(tiles, T(l, f'PTR{g}'))
                    dve.tensor_copy(pTs[g][:, :, :].rearrange("p (a k) n -> p a (k n)", a=2), pair((2, 0)[g], P, 512)).then_inc(ptr_done, 1)
                    dve.wait_ge(tiles, T(l, f'PTN{g}'))
                    dve.tensor_copy(pTn[g][:, :], ps[0:32, (6, 2)[g], 0:P]).then_inc(ptr_done, 1)

                def s_own(g):
                    dve.wait_ge(sout_mm, l * DB + 4 * g + 4)
                    dve.tensor_tensor(o_own[:, :].rearrange("p (h d) -> p h d", h=NH), ps[:, 7, :].rearrange("p (h d) -> p h d", h=NH),
                                      C('own_head').unsqueeze(2).to_broadcast([P, NH, HD]), ALU.mult).then_inc(own_done, 1)

                def s_out(g):
                    dve.wait_ge(tiles, T(l, f'SO{g}'))
                    dve.tensor_copy(cat[:, 4:8, SEQ + 16 * g:SEQ + 16 * g + 16], ps[:, 7, 0:64].rearrange("p (c n) -> p c n", c=4)).then_inc(sout_done, 1)

                hold(dve, "dve", out_nat[0], (l + 1) * 96)
                hold(dve, "dve", out_nat[1], (l + 1) * 64)
                s_logits(0)
                s_logits(1)
                s_norm(0)
                s_transposed(0)
                s_norm(1)
                s_transposed(1)

                def p_logits(n):
                    qb, c = n // 4, n % 4
                    L = (qb + 1) * P
                    if n == 0:
                        hold(dve, "dve", strip_loaded, (l + 1) * 16 * NH)
                        hold(dve, "dve", out_small, (l + 1) * 16 * OUT_SMALL + 16)
                    if n >= 2:
                        dve.wait_ge(tiles, T(l, f'PT{n - 2}'))
                    dve.wait_ge(tiles, T(l, f'PL{n}'))
                    dve.scalar_tensor_tensor(probs[:, n % 2, :, 0:L], pair(n % 2, P, L), SCALE,
                                             strip[:, 2 * c:2 * c + 2, SEQ - L:SEQ], ALU.mult, ALU.add).then_inc(plog_done, 1)
                    hold(dve, "dve", plog_done, l * 64 + 4 * n + 1)
                    mask = C('causal') if qb == 0 else work_p[:, WOFF[qb]:WOFF[qb] + L]
                    for e in range(2):
                        row = probs[:, n % 2, e, 0:L]
                        dve.tensor_tensor_reduce(out=row, in0=row, in1=mask, scale=1.0, scalar=2 * NEG, op0=ALU.add, op1=ALU.max,
                                                 accum_out=stat[:, n % 2, e:e + 1]).then_inc(plog_done, 1)
                    dve.wait_ge(plog_done, l * 64 + 4 * n + 3)
                    dve.tensor_scalar(stat[:, n % 2, 2:4], stat[:, n % 2, 0:2], -1.0, None, ALU.mult).then_inc(plog_done, 1)

                def p_norm(n):
                    L = (n // 4 + 1) * P
                    dve.wait_ge(pexp_done, l * 32 + 2 * n + 2)
                    dve.reciprocal(stat[:, n % 2, 6:8], stat[:, n % 2, 4:6]).then_inc(pnorm_done, 1)
                    dve.wait_ge(pnorm_done, l * 48 + 3 * n + 1)
                    for e in range(2):
                        row = probs[:, n % 2, e, 0:L]
                        dve.tensor_scalar(row, row, stat[:, n % 2, 6 + e:7 + e], None, ALU.mult).then_inc(pnorm_done, 1)

                for n in range(17):
                    if n == 8:
                        s_own(0)
                    if n == 9:
                        s_out(0)
                    if n < 16:
                        p_logits(n)
                    if n >= 1:
                        p_norm(n - 1)
                s_own(1)
                s_out(1)
                for c in range(KC):
                    dve.wait_ge(cathi_done, l * KC + c + 1)
                    dve.tensor_tensor(h_lo[:, c, :], cat[:, c, :], h_hi[:, c, :].bitcast(F32), ALU.subtract).then_inc(cat_ready, 1)
                for c in range(KC):
                    dve.wait_ge(tiles, T(l, f'WO{c}'))
                    dve.tensor_tensor(halves(xT[:, c, :]), pair(c % 4), halves(xT[:, c, :]), ALU.add).then_inc(x_updates, 1)
                    if c >= 2:
                        add_square(norm_no(l, 2), c - 1)
                add_square(norm_no(l, 2), KC - 1)
                ffn(l, 1)
            norm(None, 3 * DEPTH)

        @block.tensor
        def _(pe):
            ones = C('ones')
            FIRST_TOKENS = (0, P, 2 * P, 3 * P, TOK - P)

            def split_ready(l, ph, i, c):
                pe.wait_ge(units_split, unit0(l, ph) + 6 * i + c + 1 + RAW_SLOTS)

            def product(out, w0, w1, xh, xl, first, last):
                for w, x in ((w0, xh), (w0, xl), (w1, xh)):
                    for hf in range(2):
                        ins = pe.matmul(out[:, hf, :], w, x[:, HT * hf:HT * (hf + 1)],
                                        start=first and w is w0 and x is xh, stop=last and w is w1)
                return ins

            def h_chunk(before, k):
                pe.wait_ge(h_odd if k % 2 else h_ready, before // 2 + k // 2 + 1)

            def unit_tile(c, p, ks, wait_h=None, wait_cat=None, first=True, last=True):
                wh, wl = (w[:, c % 6, 0:P * len(ks)].rearrange("p (k n) -> p k n", k=len(ks)) for w in (w_hi, w_lo))
                for n, k in enumerate(ks):
                    if wait_h is not None:
                        h_chunk(wait_h, k)
                    if wait_cat is not None:
                        pe.wait_ge(cat_ready, wait_cat + k + 1)
                    ins = product(pair(p), wh[:, n, :], wl[:, n, :], h_hi[:, k, :], h_lo[:, k, :],
                                  first and n == 0, last and n == len(ks) - 1)
                return ins

            def stats(k):
                pe.wait_ge(ssum_done, (k + 1) * (KC - 1))
                for t, t0 in enumerate(FIRST_TOKENS):
                    ins = pe.matmul(ps[:, 0, t:t + 1], sq[:, 0, t0:t0 + P], ones[:, 0:1], start=True, stop=True)
                ins.then_inc(tiles, 1)

            def spread(k, p):
                pe.wait_ge(rms_done, 2 * k + 2)
                flat = rdiag[:, :, :].rearrange("p t n -> p (t n)")
                seen = SEQ - HT
                pe.matmul(pair(p)[:, 0, :], ones, flat[:, 0:HT], start=True, stop=True)
                pe.matmul(pair(p)[:, 1, 0:seen], ones, flat[:, HT:SEQ], start=True, stop=True)
                pe.matmul(pair(p)[:, 1, seen:HT], ones, flat[:, 5 * P - DB * DT:5 * P], start=True, stop=True).then_inc(rb_done, 1)

            def ffn(l, f):
                ph = 2 * f
                s0, xb, nh = (l * 2 + f) * 2 * FB, x0(l, ph), norm_no(l, ph) * KC
                stats(norm_no(l, ph))
                spread(norm_no(l, ph), 3)

                def gate_up(i, j, c0, again):
                    if not again:
                        split_ready(l, ph, j, 1)
                        for k in range(KC):
                            h_chunk(nh, k)
                            for p in range(2):
                                wh, wl = (w[:, p, P * k:P * (k + 1)] for w in (w_hi, w_lo))
                                ins = product(pair(p), wh, wl, h_hi[:, k, :], h_lo[:, k, :], k == 0, k == KC - 1)
                                if k == KC - 1:
                                    ins.then_inc(tiles, 1)
                    for p in range(0 if again else 2, 4):
                        split_ready(l, ph, j, c0 + p)
                        if again:
                            pe.wait_ge(silu_done if p < 2 else gu_done, s0 + 2 * i + p % 2 - 1)
                            pe.wait_ge(x_updates, xb + 8 * i - 11 + p)
                        unit_tile(c0 + p, p, range(KC)).then_inc(tiles, 1)

                def down(i, j, c0, final):
                    split_ready(l, ph, j, c0 + 1)
                    pe.wait_ge(act_ready, s0 + 2 * i + 2)
                    for c in range(KC):
                        p = c % 4
                        if c >= 4 or final:
                            pe.wait_ge(x_updates, xb + 8 * i + c - 3)
                        else:
                            pe.wait_ge(silu_done if p < 2 else gu_done, s0 + 2 * i + 3 + p % 2)
                        for m in range(2):
                            wh, wl = (w[:, (c0 + m) % 6, c * P:(c + 1) * P] for w in (w_hi, w_lo))
                            ins = product(pair(p), wh, wl, act_hi[:, m, :], act_lo[:, m, :], m == 0, m == 1)
                        ins.then_inc(tiles, 1)

                gate_up(0, 0, 0, False)
                with pe.Fori(0, FB - 1) as j:
                    gate_up(j + 1, j, 4, True)
                    down(j, j, 8, False)
                down(FB - 1, 0, U_FFN - 2, True)

            pe.wait_ge(s_cst, 16)
            for t in range(5):
                r = rows_of(t)
                pe.wait_ge(s_xrow[t % 2], 16 * (t // 2 + 1))
                if t == 4:
                    pe.wait_ge(x_updates, 1)
                for c in range(KC):
                    ins = pe.transpose(ps[:, 2 * (t % 4) + c // 4, P * (c % 4):P * (c % 4) + r], yst[0:r, t % 2, c * P:(c + 1) * P], ident[0:r, 0:r])
                ins.then_inc(tiles, 1)
            nv = DEPTH * 32 + 8
            pe.wait_ge(s_in, 16 * S_IN)
            pe.wait_ge(x_updates, 2)
            pe.transpose(ps[:, 2, 0:nv], vrows[0:nv, :], ident[0:nv, 0:nv]).then_inc(tiles, 1)
            pe.wait_ge(s_oh, 16)
            pe.wait_ge(x_updates, 3)
            pe.matmul(ps[0:NH, 4, :], rel_sb[:, :], oh[:, NTD:NTD + 512], start=True, stop=True)
            pe.matmul(ps[0:NH, 5, 0:NTP - 512], rel_sb[:, :], oh[:, NTD + 512:NTD + NTP], start=True, stop=True).then_inc(tiles, 1)
            pe.wait_ge(x_updates, 5)
            pe.wait_ge(zeroed, 3)
            pe.wait_ge(relx_done, 1 + 4 * DT)
            for b in range(3):
                for t in range(DT):
                    ins = pe.matmul(ps[:, b, 0:LT], relx[:, t, :], oh[:, DT - 1 - t + LT * b:DT - 1 - t + LT * (b + 1)], start=t == 0, stop=t == DT - 1)
            ins.then_inc(tiles, 1)

            pe.wait_ge(zeroed, 4)
            with pe.Fori(0, DEPTH) as l:
                ffn(l, 0)
                stats(norm_no(l, 1))
                hold(pe, "pe", st_loaded, (l + 1) * 32)
                for j in range(2):
                    pe.transpose(ps[:, 2 + j, 0:120], srow[0:120, 0, j * P:(j + 1) * P], ident[0:120, 0:120])
                    ins = pe.transpose(ps[:, 2 + j, 120:136], srow[0:16, 1, j * P:(j + 1) * P], ident[0:16, 0:16])
                ins.then_inc(tiles, 1)
                spread(norm_no(l, 1), 0)

                for q in range(2):
                    split_ready(l, 1, 0, 2 + q)
                    for m in range(4):
                        k = 4 * q + m
                        h_chunk(norm_no(l, 1) * KC, k)
                        for n in range(2):
                            wh, wl = (w[:, 2 * n + q, P * m:P * (m + 1)] for w in (w_hi, w_lo))
                            ins = product(pair(2 + n), wh, wl, h_hi[:, k, :], h_lo[:, k, :], k == 0, k == KC - 1)
                            if k == KC - 1:
                                ins.then_inc(tiles, 1)

                def z(n):
                    split_ready(l, 1, 0, n + 2)
                    unit_tile(n + 2, (n + 2) % 4, range(KC)).then_inc(tiles, 1)

                for n in range(2, 6):
                    if n == 3:
                        pe.wait_ge(st_done, l + 1)
                    if n >= 4:
                        pe.wait_ge(z_done, l * 26 + n - 3)
                    z(n)
                hold(pe, "pe", z_done, l * 26 + 6)
                for t in range(4):
                    pe.transpose(ps[:, 0, P * t:P * (t + 1)], wi[:, P * t:P * (t + 1)], ident)
                pe.matmul(ps[:, 1, 0:NEWROWS], C('head_of'), wi[:, SEQ:TOK], start=True, stop=True)
                for c in range(4):
                    ins = pe.matmul(ps[0:ID, 1, 32 * (c + 1):32 * (c + 2)], ident[64:P, 64:P], qi[64:P, c, SEQ:TOK], start=True, stop=True)
                ins.then_inc(tiles, 1)

                for n in range(12):
                    qb, c, L = 1 + n // 4, n % 4, (2 + n // 4) * P
                    if n >= 2:
                        hold(pe, "pe", relu_done, l * 12 + n - 1)
                    for e in range(2):
                        r = slice(64 * e, 64 * e + 64)
                        ins = pe.matmul(ps[:, 4 + 2 * (n % 2) + e, 0:L], qi[r, c, qb * P:(qb + 1) * P], ki[r, 0:L], start=True, stop=True)
                    ins.then_inc(tiles, 1)

                def index_keys(b):
                    if b == 0:
                        hold(pe, "pe", kidx_loaded, (l + 1) * 16 * NPG * DB)
                    hold(pe, "pe", relu_done if b < 2 else kit_done, (l * 12 + 11 + b) if b < 2 else (l * 16 + 2 * b - 3))
                    for pg in range(NPG):
                        ins = pe.transpose(ps[0:ID, 4 + 2 * (b % 2) + pg // 4, P * (pg % 4):P * (pg % 4) + P], kipages[:, b, pg, :], ident)
                    ins.then_inc(tiles, 1)

                index_keys(0)
                for b in range(DB):
                    if b < DB - 1:
                        index_keys(b + 1)
                    if b == 0:
                        hold(pe, "pe", wt_done, l * 6 + 6)
                    if b == 4:
                        hold(pe, "pe", srelu_done, l * 2 + 1)
                    hold(pe, "pe", kit_done, l * 16 + 2 * b + 2)
                    r = 32 * (b % 4)
                    for t in range(3):
                        ins = pe.matmul(ps[r:r + 32, t, 0:LT], qis[:, b, :], kidxT[:, b % 2, LT * t:LT * (t + 1)], start=True, stop=True)
                    ins.then_inc(score_mm, 1)
                hold(pe, "pe", srelu_done, l * 2 + 2)
                for t in range(3):
                    for g in range(2):
                        ins = pe.matmul(ps[0:32, 4 + t, 0:LT], wsel[:, g, :], srelu[:, g, t, :], start=g == 0, stop=g == 1)
                ins.then_inc(tiles, 1)

                def tail(j):
                    hold(pe, "pe", ucx_done, l * 2 + j + 1)
                    pe.transpose(ps[0:47, 0, 0:P], cz[:, 3, TAIL:TOK], ident)
                    pe.transpose(ps[0:6 * DB, 1, 0:P], ucx[:, 2 + SEQ:NUX], ident)
                    pe.transpose(ps[0:2, 1, P:2 * P], ucx[:, SEQ:SEQ + 2], ident).then_inc(tiles, 1)

                def pool_product(j):
                    hold(pe, "pe", pw_loaded, (l + 1) * 64)
                    hold(pe, "pe", d_done, l * 2 + j + 1)
                    for hf in range(2):
                        ins = pe.matmul(pair(1)[:, hf, :], pw[:, j, :], pb[0][:, HT * hf:HT * (hf + 1)], start=True, stop=True)
                    ins.then_inc(tiles, 1)

                for n in range(6, 18):
                    if n in (8, 9):
                        pe.wait_ge(sc_done, l + 1)
                    if n >= 10:
                        pe.wait_ge(z_done, l * 26 + n - 3)
                    z(n)
                hold(pe, "pe", z_done, l * 26 + 16)
                tail(0)
                pool_product(0)
                for n in range(18, 26):
                    if n == 18:
                        pe.wait_ge(tail_done, l * 6 + 3)
                    elif n == 19:
                        pe.wait_ge(pm_done, l * 2 + 1)
                    else:
                        pe.wait_ge(z_done, l * 26 + n - 3)
                    z(n)
                hold(pe, "pe", z_done, l * 26 + 26)
                for t in range(5):
                    r = rows_of(t)
                    ins = pe.transpose(ps[0:r, 0, ID * t:ID * (t + 1)], ki[0:ID, P * t:P * t + r], ident[0:ID, 0:ID])
                ins.then_inc(tiles, 1)
                for t in range(5):
                    r, bank = rows_of(t), 2 * ((t + 1) % 4)
                    if t == 3:
                        hold(pe, "pe", kin_done, l * 2 + 2)
                    if t == 4:
                        hold(pe, "pe", nat_done, l * 10 + 2)
                    for q, src in enumerate((kT, v_sb)):
                        for c in range(4):
                            ins = pe.transpose(ps[0:r, bank + q, P * c:P * (c + 1)], src[:, c, P * t:P * t + r], ident)
                    ins.then_inc(tiles, 1)

                def key_tile(b, j):
                    m = 4 * b + j
                    if m < 2:
                        hold(pe, "pe", nat_done, l * 10 + 4 + 2 * m)
                    elif j % 2:
                        hold(pe, "pe", keys_odd, l * 16 + 2 * ((m - 2) // 4) + (m - 2) % 4 // 2 + 1)
                    else:
                        hold(pe, "pe", keys_done, l * 24 + 3 * ((m - 2) // 4) + (m - 2) % 4 // 2 + 1)
                    if j % 2 == 0:
                        hold(pe, "pe", k_loaded[b % 2][j // 2], l * 4 * 64 + (b // 2 + 1) * 64)
                    for pg in (2 * j, 2 * j + 1):
                        for c in range(4):
                            col = 256 * (c % 2) + P * (pg % 2)
                            ins = pe.transpose(ps[:, 4 + 2 * (j % 2) + c // 2, col:col + P], kpages[b % 2][:, pg, P * c:P * (c + 1)], ident)
                    ins.then_inc(tiles, 1)

                def logits(b):
                    if b == 0:
                        hold(pe, "pe", qz_done, (l + 1) * NH)
                        hold(pe, "pe", keys_padded, l + 1)
                        hold(pe, "pe", nat_done, (l + 1) * 10)
                    if b == 4:
                        hold(pe, "pe", pm_done, l * 2 + 2)
                    hold(pe, "pe", keys_done, l * 24 + 3 * b + 3)
                    hold(pe, "pe", keys_odd, l * 16 + 2 * b + 2)
                    r = 32 * (b % 4)
                    for t in range(3):
                        for c in range(4):
                            ins = pe.matmul(ps[r:r + 32, t, 0:LT], qz[:, c, b, :], keysT[:, c, LT * t:LT * (t + 1)], start=c == 0, stop=c == 3)
                        ins.then_inc(logit_mm, 1)

                for j in range(4):
                    key_tile(0, j)
                for b in range(DB):
                    if b < DB - 1:
                        key_tile(b + 1, 0)
                        key_tile(b + 1, 1)
                    logits(b)
                    if b == 3:
                        hold(pe, "pe", lg_done, l * 2 + 1)
                        tail(1)
                        pool_product(1)
                    if b < DB - 1:
                        key_tile(b + 1, 2)
                        key_tile(b + 1, 3)
                hold(pe, "pe", masks_done, l * 3 + 2)
                hold(pe, "pe", lg_done, l * 2 + 2)
                for g in range(2):
                    for t in range(3):
                        ins = pe.matmul(ps[:, (4, 0)[g] + t, 0:LT], C('row_of', 32, P, P * g), work_s[:, LT * t:LT * (t + 1)], start=True, stop=True)
                    ins.then_inc(tiles, 1)

                for g in range(2):
                    hold(pe, "pe", snorm_done, l * 6 + 3 * g + 3)
                    for pg in range(NPG):
                        ins = pe.transpose(ps[:, (4, 0)[g] + pg // 4, P * (pg % 4):P * (pg % 4) + P], lg[:, g, P * pg:P * (pg + 1)], ident)
                    ins.then_inc(tiles, 1)
                    pe.transpose(ps[0:32, (6, 2)[g], 0:P], pnew[:, :], ident).then_inc(tiles, 1)

                def values(b):
                    g, q = b // 4, b % 4
                    if q == 0:
                        hold(pe, "pe", ptr_done, l * 4 + 2 * g + 2)
                    if b == 4:
                        hold(pe, "pe", sout_done, l * 2 + 1)
                    hold(pe, "pe", v_loaded[b % 3], l * (3, 3, 2)[b % 3] * 16 * NPG + (b // 3 + 1) * 16 * NPG)
                    out, mine = ps[32 * q:32 * q + 32, 7, :], slice(32 * q, 32 * q + 32)
                    for pg in range(NPG):
                        pe.matmul(out, pTs[g][:, pg, mine], vpages[b % 3][:, pg, :], start=pg == 0, stop=False)
                    pe.matmul(out, pTn[g][:, mine], vn[0:NEWROWS, 4, :], start=False, stop=True).then_inc(sout_mm, 1)

                def own_outputs(g):
                    hold(pe, "pe", own_done, l * 2 + g + 1)
                    for c in range(4):
                        ins = pe.matmul(ps[:, 7, 16 * c:16 * c + 16], o_own[:, P * c:P * (c + 1)], C('out_of'), start=True, stop=True)
                    ins.then_inc(tiles, 1)

                def prompt_logits(n):
                    qb, c, L = n // 4, n % 4, (n // 4 + 1) * P
                    if n >= 2:
                        hold(pe, "pe", plog_done, l * 64 + 4 * (n - 2) + 1)
                    for e in range(2):
                        r = slice(64 * e, 64 * e + 64)
                        ins = pe.matmul(pair(n % 2, P, L)[:, e, :], qT[r, c, qb * P:(qb + 1) * P], kT[r, c, 0:L], start=True, stop=True)
                    ins.then_inc(tiles, 1)

                hold(pe, "pe", ptr_done, l * 4 + 4)
                prompt_logits(0)
                for n in range(18):
                    if n in V_AT:
                        values(V_AT[n])
                    if n < 15:
                        prompt_logits(n + 1)
                    if 1 <= n < 17:
                        m = n - 1
                        hold(pe, "pe", pnorm_done, l * 48 + 3 * m + 3)
                        if m >= 1:
                            hold(pe, "pe", ppt_done, l * 16 + m)
                        for e in range(2):
                            for kb in range(m // 4 + 1):
                                ins = pe.transpose(ps[:, 4 + e, P * kb:P * (kb + 1)], probs[:, m % 2, e, P * kb:P * (kb + 1)], ident)
                        ins.then_inc(tiles, 1)
                    if n >= 2:
                        m = n - 2
                        hold(pe, "pe", ppt_done, l * 16 + m + 1)
                        if m >= 1:
                            hold(pe, "pe", po_done, l * 16 + m)
                        for e in range(2):
                            h = 2 * (m % 4) + e
                            for kb in range(m // 4 + 1):
                                ins = pe.matmul(ps[64 * e:64 * e + 64, 6, 0:P], vn[:, kb, HD * h:HD * (h + 1)], pTp[:, e, P * kb:P * (kb + 1)],
                                                start=kb == 0, stop=kb == m // 4)
                        ins.then_inc(tiles, 1)
                    if n == 8:
                        own_outputs(0)
                own_outputs(1)

                for n in range(8):
                    split_ready(l, 1, 0, 28 + n)
                    if n >= 4:
                        pe.wait_ge(x_updates, x0(l, 1) + n - 3)
                    unit_tile(28 + n, n % 4, range(KC), wait_cat=None if n else l * KC).then_inc(tiles, 1)
                ffn(l, 1)

            stats(3 * DEPTH)
            spread(3 * DEPTH, 3)
            pe.wait_ge(hhi_done, (3 * DEPTH + 1) * KC)
            for t in range(5):
                r = rows_of(t)
                if t == 4:
                    pe.wait_ge(y_done, 1)
                for c in range(KC):
                    ins = pe.transpose(ps[0:r, 2 * (t % 4) + c // 4, P * (c % 4):P * (c % 4) + P], yT[:, c, t * P:t * P + r], ident)
                ins.then_inc(tiles, 1)


_INS = ['x_prompt', 'x_sample', 'cache_k', 'cache_v', 'cache_kidx', 'state_conv', 'state_pool', 'page_table',
        'norm_ffn1', 'ffn1_gate', 'ffn1_up', 'ffn1_down', 'norm_mix', 'w_in', 'conv_w', 'pool_w', 'pool_scale', 'w_o',
        'norm_ffn2', 'ffn2_gate', 'ffn2_up', 'ffn2_down', 'rel_bias', 'norm_final']
_OUTS = [('y_prompt', (1, SEQ, D)), ('y_sample', (DB, DT, D)),
         ('k_prompt', (DEPTH, 1, SEQ, NH, HD)), ('v_prompt', (DEPTH, 1, SEQ, NH, HD)), ('kidx_prompt', (DEPTH, 1, SEQ, ID)),
         ('conv_prompt', (DEPTH, 1, 2, WC)), ('pool_prompt', (DEPTH, 1, 15, WP)),
         ('k_sample', (DEPTH, DB, DT, NH, HD)), ('v_sample', (DEPTH, DB, DT, NH, HD)), ('kidx_sample', (DEPTH, DB, DT, ID)),
         ('conv_sample', (DEPTH, DB, 2, WC)), ('pool_sample', (DEPTH, DB, 15, WP))]


def kernel(**inputs):
    import concourse.bacc as _bacc
    from concourse.bass_utils import run_bass_kernel_spmd as _run

    nc = _bacc.Bacc("TRN2", target_bir_lowering=False, num_devices=1)
    arrays, aps = {}, {}
    given = {n: np.ascontiguousarray(inputs[n]) for n in _INS}
    given['consts'] = shape_constants()
    given['onehots'] = bucket_one_hots()
    for name, v in given.items():
        arrays[f"in_{name}"] = v
        aps[name] = nc.dram_tensor(f"in_{name}", v.shape, mybir.dt.from_np(v.dtype), kind="ExternalInput").ap()
    for name, shape in _OUTS:
        aps[name] = nc.dram_tensor(f"out_{name}", shape, F32, kind="ExternalOutput").ap()
    aps['scratch'] = nc.dram_tensor("bias_by_distance", (NH, P, NTP), F32, kind="Internal").ap()
    trunk(nc, aps)
    r = _run(nc, [arrays], core_ids=[0])
    return tuple(r.results[0][f"out_{name}"] for name, _ in _OUTS)
```
